# Optimizing a Trainium2 kernel written in Bass

```python
import math
import jax, jax.numpy as jnp
from jax import lax
import numpy as np

D_MODEL = 1024
BATCH = 1
SEQ = 1024
DEPTH = 2
DEC_BATCH = 1
DEC_SEQ = 1024
PAST_LEN = 128

N_MIXERS = 2
EPS = 1e-6
ATTN_GROUPS = ((128, 1), (512, 4), (2048, 16))
N_GROUPS = len(ATTN_GROUPS)
HEADS_PER_GROUP = 8
ATTN_HEAD_DIM = 64
GROUP_WIDTH = HEADS_PER_GROUP * ATTN_HEAD_DIM
A_IN_WIDTH = 3 * N_GROUPS * GROUP_WIDTH + GROUP_WIDTH
NUM_BUCKETS = 32
MAX_DISTANCE = 1024
NEG_INF = -1e30
DN_HEADS = 8
DN_HEAD_DIM = 128
DN_WIDTH = DN_HEADS * DN_HEAD_DIM
CONV_K = 5
CHUNK = 64
B_IN_WIDTH = 4 * DN_WIDTH + 4 * DN_HEADS
N_A_LAYERS = (DEPTH + 1) // 2
N_B_LAYERS = DEPTH // 2

kernel_name = 'hybrid_dilated_attn_gated_deltanet_encoder'

def rms_norm(x, w):
    xf = x.astype(jnp.float32)
    y = xf * lax.rsqrt(jnp.mean(xf * xf, axis=-1, keepdims=True) + EPS)
    return (y * w.astype(jnp.float32)).astype(x.dtype)

def t5_bucket(rel):
    nb = NUM_BUCKETS // 2
    max_exact = nb // 2
    ret = (rel > 0).astype(np.int32) * nb
    n = np.abs(rel)
    large = max_exact + (np.log(np.maximum(n, 1) / max_exact) / math.log(MAX_DISTANCE / max_exact)
                         * (nb - max_exact)).astype(np.int32)
    large = np.minimum(large, nb - 1)
    return ret + np.where(n < max_exact, n, large).astype(np.int32)

def group_bias(rel_bias_g, dil, half):
    W = half
    qq = np.arange(W)[:, None]
    kk = np.arange(3 * W)[None, :]
    rel = (kk - W - qq) * dil
    bucket = t5_bucket(rel)
    return jnp.transpose(rel_bias_g.astype(jnp.float32)[bucket], (2, 0, 1))

def residue_split(t, dil):
    B, S = t.shape[0], t.shape[1]
    t = t.reshape(B, S // dil, dil, *t.shape[2:])
    t = jnp.moveaxis(t, 2, 1)
    return t.reshape(B * dil, S // dil, *t.shape[3:])

def residue_merge(t, B, dil):
    L = t.shape[1]
    t = t.reshape(B, dil, L, *t.shape[2:])
    t = jnp.moveaxis(t, 1, 2)
    return t.reshape(B, L * dil, *t.shape[3:])

def banded_attention(q, k, v, bias, half):
    Bd, L, H, hd = q.shape
    W = half
    nb = -(-L // W)
    Lp = nb * W
    pq = Lp - L
    qp = jnp.pad(q, ((0, 0), (0, pq), (0, 0), (0, 0))).reshape(Bd, nb, W, H, hd)

    def key_blocks(t):
        tp = jnp.pad(t, ((0, 0), (W, pq + W), (0, 0), (0, 0))).reshape(Bd, nb + 2, W, H, hd)
        return jnp.concatenate([tp[:, :-2], tp[:, 1:-1], tp[:, 2:]], axis=2)

    kb, vb = key_blocks(k), key_blocks(v)
    s = jnp.einsum('bnqhd,bnkhd->bnhqk', qp, kb, preferred_element_type=jnp.float32)
    s = s * (hd ** -0.5) + bias[None, None]
    kidx = np.arange(nb)[:, None] * W + np.arange(3 * W)[None, :] - W
    kvalid = (kidx >= 0) & (kidx < L)
    band = np.abs(np.arange(3 * W)[None, :] - W - np.arange(W)[:, None]) <= half
    mask = kvalid[:, None, None, :] & band[None, None, :, :]
    s = jnp.where(mask[None], s, NEG_INF)
    m = jnp.max(s, axis=-1, keepdims=True)
    p = jnp.exp(s - m)
    l = jnp.sum(p, axis=-1)
    o = jnp.einsum('bnhqk,bnkhd->bnqhd', p, vb.astype(jnp.float32))
    o = o / jnp.transpose(l, (0, 1, 3, 2))[..., None]
    lse = jnp.transpose(m[..., 0] + jnp.log(l), (0, 1, 3, 2))
    o = o.reshape(Bd, Lp, H, hd)[:, :L]
    lse = lse.reshape(Bd, Lp, H)[:, :L]
    return o, lse

def dilated_attention_mixer(h, w_in, w_out, rel_bias):
    B, S, _ = h.shape
    proj = h @ w_in
    z = proj[..., 3 * N_GROUPS * GROUP_WIDTH:]
    outs, lses = [], []
    for g, (win, dil) in enumerate(ATTN_GROUPS):
        base = 3 * g * GROUP_WIDTH
        shp = (B, S, HEADS_PER_GROUP, ATTN_HEAD_DIM)
        q = proj[..., base:base + GROUP_WIDTH].reshape(shp)
        k = proj[..., base + GROUP_WIDTH:base + 2 * GROUP_WIDTH].reshape(shp)
        v = proj[..., base + 2 * GROUP_WIDTH:base + 3 * GROUP_WIDTH].reshape(shp)
        half = win // (2 * dil)
        bias = group_bias(rel_bias[:, g * HEADS_PER_GROUP:(g + 1) * HEADS_PER_GROUP], dil, half)
        o, lse = banded_attention(residue_split(q, dil), residue_split(k, dil),
                                  residue_split(v, dil), bias, half)
        outs.append(residue_merge(o, B, dil))
        lses.append(residue_merge(lse, B, dil))
    wts = jax.nn.softmax(jnp.stack(lses, 0), axis=0)
    o = jnp.einsum('gbsh,gbshd->bshd', wts, jnp.stack(outs, 0))
    o = o.reshape(B, S, GROUP_WIDTH).astype(h.dtype) * jax.nn.silu(z)
    return o @ w_out

def centred_conv(x, w):
    C = x.shape[-1]
    K = w.shape[0]
    return lax.conv_general_dilated(x, w.astype(x.dtype).reshape(K, 1, C), window_strides=(1,),
                                    padding=((K // 2, K // 2),),
                                    dimension_numbers=('NWC', 'WIO', 'NWC'),
                                    feature_group_count=C)

def l2_normalize(x):
    return x * lax.rsqrt(jnp.sum(x * x, axis=-1, keepdims=True) + EPS)

def chunk_gated_delta(q, k, v, beta, g):
    B, S, H, DK = q.shape
    DV = v.shape[-1]
    N = S // CHUNK

    def to_chunks(t):
        t = t.reshape(B, N, CHUNK, H, *t.shape[3:])
        return jnp.moveaxis(t, 3, 1)

    qc, kc, vc = to_chunks(q), to_chunks(k), to_chunks(v)
    bc = to_chunks(beta)
    gc = jnp.cumsum(to_chunks(g), axis=-1)
    tril = np.tril(np.ones((CHUNK, CHUNK), dtype=bool))
    strict = np.tril(np.ones((CHUNK, CHUNK), dtype=bool), -1)
    diff = gc[..., :, None] - gc[..., None, :]
    decay = jnp.where(tril, jnp.exp(jnp.where(tril, diff, 0.0)), 0.0)
    kb = kc * bc[..., None]
    vb = vc * bc[..., None]
    A = jnp.where(strict, jnp.einsum('bhncd,bhnsd->bhncs', kb, kc) * decay, 0.0)
    rhs = jnp.concatenate([vb, kb * jnp.exp(gc)[..., None]], axis=-1)
    sol = lax.linalg.triangular_solve(A, rhs, left_side=True, lower=True, unit_diagonal=True)
    u, w = sol[..., :DV], sol[..., DV:]
    qk = jnp.where(tril, jnp.einsum('bhncd,bhnsd->bhncs', qc, kc) * decay, 0.0)
    q_dec = qc * jnp.exp(gc)[..., None]
    g_last = gc[..., -1]
    k_dec = kc * jnp.exp(g_last[..., None] - gc)[..., None]

    def step(state, xs):
        qk_i, qd_i, w_i, u_i, kd_i, gl_i = xs
        v_new = u_i - jnp.einsum('bhcd,bhde->bhce', w_i, state)
        out = jnp.einsum('bhcd,bhde->bhce', qd_i, state) + jnp.einsum('bhcs,bhse->bhce', qk_i, v_new)
        state = state * jnp.exp(gl_i)[..., None, None] + jnp.einsum('bhcd,bhce->bhde', kd_i, v_new)
        return state, out

    xs = tuple(jnp.moveaxis(t, 2, 0) for t in (qk, q_dec, w, u, k_dec, g_last))
    state0 = jnp.zeros((B, H, DK, DV), jnp.float32)
    _, out = lax.scan(step, state0, xs)
    out = jnp.transpose(out, (1, 0, 3, 2, 4))
    return out.reshape(B, S, H, DV)

def gated_deltanet_mixer(h, w_in, conv_w, A_log, dt_bias, out_norm_w, w_out):
    B, S, _ = h.shape
    proj = h @ w_in
    qkv = jax.nn.silu(centred_conv(proj[..., :3 * DN_WIDTH], conv_w))
    z = proj[..., 3 * DN_WIDTH:4 * DN_WIDTH]
    a = proj[..., 4 * DN_WIDTH:4 * DN_WIDTH + 2 * DN_HEADS].reshape(B, S, 2, DN_HEADS).astype(jnp.float32)
    b = proj[..., 4 * DN_WIDTH + 2 * DN_HEADS:].reshape(B, S, 2, DN_HEADS).astype(jnp.float32)
    qkv = qkv.astype(jnp.float32)
    shp = (B, S, DN_HEADS, DN_HEAD_DIM)
    q = l2_normalize(qkv[..., :DN_WIDTH].reshape(shp)) * (DN_HEAD_DIM ** -0.5)
    k = l2_normalize(qkv[..., DN_WIDTH:2 * DN_WIDTH].reshape(shp))
    v = qkv[..., 2 * DN_WIDTH:].reshape(shp)
    beta = jax.nn.sigmoid(b)
    g = -jnp.exp(A_log.astype(jnp.float32)) * jax.nn.softplus(a + dt_bias.astype(jnp.float32))
    o_fwd = chunk_gated_delta(q, k, v, beta[:, :, 0], g[:, :, 0])
    o_bwd = chunk_gated_delta(q[:, ::-1], k[:, ::-1], v[:, ::-1],
                              beta[:, ::-1, 1], g[:, ::-1, 1])[:, ::-1]
    o = o_fwd + o_bwd
    o = o * lax.rsqrt(jnp.mean(o * o, axis=-1, keepdims=True) + EPS) * out_norm_w.astype(jnp.float32)
    o = o.reshape(B, S, DN_WIDTH).astype(h.dtype) * jax.nn.silu(z)
    return o @ w_out

def trunk(x, norm_w, final_norm_w, rel_bias, a_w_in, a_w_out, b_w_in, b_conv_w,
          b_A_log, b_dt_bias, b_out_norm_w, b_w_out):
    for i in range(DEPTH):
        h = rms_norm(x, norm_w[i])
        j = i // N_MIXERS
        if i % N_MIXERS == 0:
            x = x + dilated_attention_mixer(h, a_w_in[j], a_w_out[j], rel_bias)
        else:
            x = x + gated_deltanet_mixer(h, b_w_in[j], b_conv_w[j], b_A_log[j], b_dt_bias[j],
                                         b_out_norm_w[j], b_w_out[j])
    return rms_norm(x, final_norm_w)

def setup_inputs(seed: int = 0) -> dict:
    key = jax.random.key(seed)
    ks = jax.random.split(key, 16)
    f32 = jnp.float32
    x_prompt = jax.random.normal(ks[0], (BATCH, SEQ, D_MODEL), f32)
    x_sample = jax.random.normal(ks[1], (DEC_BATCH, DEC_SEQ, D_MODEL), f32)
    norm_w = 1.0 + 0.1 * jax.random.normal(ks[2], (DEPTH, D_MODEL), f32)
    final_norm_w = 1.0 + 0.1 * jax.random.normal(ks[3], (D_MODEL,), f32)
    rel_bias = 0.5 * jax.random.normal(ks[4], (NUM_BUCKETS, N_GROUPS * HEADS_PER_GROUP), f32)
    a_w_in = jax.random.normal(ks[5], (N_A_LAYERS, D_MODEL, A_IN_WIDTH), f32) * D_MODEL ** -0.5
    a_w_out = jax.random.normal(ks[6], (N_A_LAYERS, GROUP_WIDTH, D_MODEL), f32) * GROUP_WIDTH ** -0.5
    b_w_in = jax.random.normal(ks[7], (N_B_LAYERS, D_MODEL, B_IN_WIDTH), f32) * D_MODEL ** -0.5
    b_conv_w = jax.random.normal(ks[8], (N_B_LAYERS, CONV_K, 3 * DN_WIDTH), f32) * CONV_K ** -0.5
    b_A_log = jnp.log(jax.random.uniform(ks[9], (N_B_LAYERS, 2, DN_HEADS), f32, 1.0, 16.0))
    dt = jnp.exp(jax.random.uniform(ks[10], (N_B_LAYERS, 2, DN_HEADS), f32,
                                    math.log(1e-3), math.log(1e-1)))
    b_dt_bias = dt + jnp.log(-jnp.expm1(-dt))
    b_out_norm_w = 1.0 + 0.1 * jax.random.normal(ks[11], (N_B_LAYERS, DN_HEAD_DIM), f32)
    b_w_out = jax.random.normal(ks[12], (N_B_LAYERS, DN_WIDTH, D_MODEL), f32) * DN_WIDTH ** -0.5
    return {'x_prompt': x_prompt, 'x_sample': x_sample, 'norm_w': norm_w,
            'final_norm_w': final_norm_w, 'rel_bias': rel_bias, 'a_w_in': a_w_in,
            'a_w_out': a_w_out, 'b_w_in': b_w_in, 'b_conv_w': b_conv_w, 'b_A_log': b_A_log,
            'b_dt_bias': b_dt_bias, 'b_out_norm_w': b_out_norm_w, 'b_w_out': b_w_out}

def reference(x_prompt, x_sample, norm_w, final_norm_w, rel_bias, a_w_in, a_w_out, b_w_in,
              b_conv_w, b_A_log, b_dt_bias, b_out_norm_w, b_w_out):
    y_prompt = trunk(x_prompt, norm_w, final_norm_w, rel_bias, a_w_in, a_w_out, b_w_in,
                     b_conv_w, b_A_log, b_dt_bias, b_out_norm_w, b_w_out)
    y_sample = trunk(x_sample, norm_w, final_norm_w, rel_bias, a_w_in, a_w_out, b_w_in,
                     b_conv_w, b_A_log, b_dt_bias, b_out_norm_w, b_w_out)
    return (y_prompt, y_sample)


_drawn_inputs = setup_inputs


def setup_inputs(seed=0):
    import zlib

    import numpy as np

    out = dict(_drawn_inputs(seed))
    spreads = {}
    factors = {}
    for name, (base, spread) in spreads.items():
        noise = np.random.default_rng([zlib.crc32(name.encode()), seed]).standard_normal(out[name].shape)
        drawn = base * np.exp(spread * noise) if base else spread * noise
        out[name] = __import__('jax').numpy.asarray(drawn.astype(out[name].dtype))
    for name, factor in factors.items():
        out[name] = (out[name] * factor).astype(out[name].dtype)
    return out
```

```python
from contextlib import ExitStack

import numpy as np
import concourse.bass as bass
from concourse import mybir

F32 = mybir.dt.float32
F32R = mybir.dt.float32r
ALU = mybir.AluOpType
ACT = mybir.ActivationFunctionType
AX = mybir.AxisListType

P = 128
SEQS = 2
S = 1024
D = 1024
KD = D // P
HALF = 512
EPS = 1e-6
NEG = -1e30

GROUPS = ((128, 1), (512, 4), (2048, 16))
NG = 3
HEADS = 8
HD = 64
PAIRS = HEADS // 2
SCALE = HD ** -0.5
BAND = 64
REL = 384
REL0 = 191
NUM_BUCKETS = 32
QT = S // P
OC = P + 4
SLOTS = (1, 2, 0)

DH = 8
CONV_K = 5
PAD = CONV_K // 2
NC = S // P
DIRS = 2
NU = NC * DIRS
BLK = 32
NB = P // BLK
LANES = NB * NU
TINY = 1e-30
G_STEPS, G_ACTS = 18, 9
SUB_STEPS = 2 * (BLK - 2)
GSGN, EG, KDX, EGL, NBETA, COEF, BETA = range(7)
NK = 7

KC_A = 4
A_TILES = 10 * PAIRS
O_TILES = D // P
B0 = A_TILES + O_TILES
B_TILES = 4 * DH
STREAM = B0 + B_TILES + O_TILES
W_BUFS = 2
ARENA = 28984
FILL0 = (0, 3, 5)
O_OF = (3, 2, 0)


def runs(ns):
    out, a = [], 0
    for b in range(1, len(ns) + 1):
        if b == len(ns) or ns[b] != ns[a]:
            out.append((a, b))
            a = b
    return out


def q_tile(g, t):
    if g == 2:
        return P * t, P * t, 0, P
    q0 = P * t
    first = t == 0 if g == 0 else t % 2 == 0
    last = t == QT - 1 if g == 0 else t % 2 == 1
    return q0, q0 - BAND, BAND if first else 0, 3 * BAND if last else 4 * BAND


def v_tiles(g):
    if g == 2:
        return [(P * t, P) for t in range(QT)]
    span = S if g == 0 else S // 4
    out = []
    for c in range(0, S, span):
        out += [(c, BAND)] + [(c + BAND + P * j, P) for j in range(span // P - 1)]
        out += [(c + span - BAND, BAND)]
    return out


def chunks(g, t):
    _, _, lo, hi = q_tile(g, t)
    if g == 2:
        return [(0, P, t)]
    v0 = t if g == 0 else (t // 2) * 3 + t % 2
    return [(max(lo, P * c), min(hi, P * c + P) - max(lo, P * c), v0 + c) for c in range(2)]


def in_group_order(buf, bank, g, n):
    dil = GROUPS[g][1]
    if dil == 1:
        return buf[:, HALF * n:HALF * n + HALF], bank[:, :]
    per = HALF // dil
    return (buf.rearrange("p (r l) -> p l r", r=dil)[:, per * n:per * n + per, :],
            bank.rearrange("p (l r) -> p l r", r=dil))


def program(nc, xT, wA, woA, wB, norm_w, rel_bias, onehot, d_outband, d_ident, d_ones, d_conv_w,
            d_wab, d_a_log, d_dt, d_onorm, d_tri, d_masks, yT):
    ctx = ExitStack()
    with ctx:
        def sb(name, shape, dt=F32):
            return ctx.enter_context(nc.sbuf_tensor(name, shape, dt))

        def sem(name):
            return ctx.enter_context(nc.semaphore(name))

        bias_rows = nc.dram_tensor("bias_rows", (NG * HEADS, REL), F32, kind="Internal")
        xch = [nc.dram_tensor(f"xch{g}", (S, OC), F32, kind="Internal").ap() for g in (1, 2)]

        bias_copies = nc.dram_tensor("bias_copies", (NG * HEADS, P, REL), F32, kind="Internal")
        x1T = nc.dram_tensor("x1T", (SEQS, P, KD, S), F32, kind="Internal").ap()
        gate_rows = nc.dram_tensor("gate_rows", (DIRS * DH, NC, P), F32, kind="Internal").ap()
        blocks = nc.dram_tensor("blocks", (NB, NU, BLK, BLK), F32, kind="Internal").ap()
        inverses = nc.dram_tensor("inverses", (NB, NU, BLK, BLK), F32, kind="Internal").ap()
        headsT = nc.dram_tensor("headsT", (DH, P, S), F32, kind="Internal").ap()

        h_hi = sb("h_hi", [P, KD, S], F32R)
        h_lo = sb("h_lo", [P, KD, S], F32R)
        w_raw = sb("w_raw", [P, W_BUFS, KD * P])
        w_hi = sb("w_hi", [P, W_BUFS, KD * P], F32R)
        w_lo = sb("w_lo", [P, W_BUFS, KD * P], F32R)
        ident = sb("ident", [P, P])
        ones = sb("ones", [P, P])
        eps_c = sb("eps_c", [P, 2])
        conv_w = sb("conv_w", [P, 3, DH, CONV_K])
        wab = sb("wab", [P, KD, 4 * DH])
        a_log = sb("a_log", [P, DIRS * DH])
        dt_b = sb("dt_b", [P, DIRS * DH])
        onorm = sb("onorm", [P, 1])
        tri = sb("tri", [P, DIRS, P])
        masks = sb("masks", [P, 3, P])
        normw = sb("normw", [P, 3, KD])
        arena = sb("arena", [P, ARENA])
        used = [0]

        def take(*shape):
            n = int(np.prod(shape))
            v = arena[:, used[0]:used[0] + n]
            used[0] += n
            if len(shape) > 1:
                names = "abcd"[:len(shape)]
                v = v.rearrange(f"p ({' '.join(names)}) -> p {' '.join(names)}",
                                **dict(zip(names, shape)))
            return v

        bias01 = [take(HEADS, 4 * BAND), take(HEADS, 4 * BAND)]
        bias2 = take(HEADS, P)
        q_sb = take(3, 2, S)
        k0 = used[0]
        k_sb = take(3, S)
        v_ch = take(S)
        v_nat = take(12, P)
        s_sb = take(2, 2, 4 * BAND)
        p_t = take(2, 4 * P)
        o_sb = take(4, QT, OC)
        zs = take(S)
        o_end = used[0]
        wgt = take(5, 3, QT, 2)
        o_all = take(PAIRS, S)
        assert used[0] <= ARENA
        early = o_all.rearrange("p h t -> p (h t)")
        oneh = early[0:NUM_BUCKETS, 0:NG * REL].rearrange("p (g r) -> p g r", g=NG)
        rows = early[0:HEADS, NG * REL:2 * NG * REL].rearrange("p (g r) -> p g r", g=NG)
        outband = early[0:HEADS, 2 * NG * REL:(2 * NG + 1) * REL]
        relb = early[0:NUM_BUCKETS, (2 * NG + 1) * REL:(2 * NG + 1) * REL + NG * HEADS]
        used[0] = k0
        x_sb = take(KD, S)
        sq = take(2, S)
        sumsq = take(S)
        rstd = take(S)
        assert used[0] <= o_end
        used[0] = 0
        gates = take(NK * DIRS, DH, NC)
        gate_h = take(NK, DIRS, NC)
        conv_h = take(3, CONV_K)
        gt = take(9, DIRS * DH * NC)
        state = take(DIRS, P)
        rhs = take(DIRS, P)
        v_new = take(DIRS, P)
        rnorm = take(2, NC)
        orms = take(NC)
        raw = take(3, S + 2 * PAD)
        z_raw = take(S)
        z_silu = take(S)
        kdec = take(DIRS, NC, P)
        assert used[0] <= ARENA
        vv = take(DIRS, NC, P)
        nat = take(2, NC, P)
        kq = take(NC, 2, P)
        low0 = used[0]
        low = take(NU, P)
        low1_0 = used[0]
        low1 = take(NU, P)
        decay = take(NU, P)
        qkt = take(NU, P)
        inv_t0 = used[0]
        inv_t = take(NU, P)
        xm = take(NU, P)
        assert used[0] <= ARENA, used[0]
        inv = decay
        used[0] = low1_0
        o_dir = take(DIRS, NC, P)
        used[0] = low0
        sq_h = take(2, S)
        used[0] = inv_t0
        lanes = take(BLK, BLK)
        ltmp = take(BLK, BLK)
        qkm = take(NC, P)
        oT_h = take(S)
        cv = [nat[:, i, :, :].rearrange("p c t -> p (c t)") for i in range(2)]
        cv.append(qkm.rearrange("p c t -> p (c t)"))
        psum = [ctx.enter_context(nc.psum_tensor(f"bank{i}", [P, HALF], F32)) for i in range(8)]
        ps_proj, ps_s, ps_pt, ps_o, ps_v = psum[0:2], psum[2:4], psum[4], psum[5], psum[6:8]

        const_loaded = sem("const_loaded")
        rows_done = sem("rows_done")
        rows_copied = sem("rows_copied")
        rows_stored = sem("rows_stored")
        bias_loaded = sem("bias_loaded")
        x_loaded = [sem(f"x_loaded{k}") for k in range(KD)]
        squared = sem("squared")
        summed = sem("summed")
        sumsq_done = sem("sumsq_done")
        rstd_done = sem("rstd_done")
        rms_done = sem("rms_done")
        h_scaled = sem("h_scaled")
        h_hi_done = sem("h_hi_done")
        h_lo_dve = sem("h_lo_dve")
        h_lo_pool = sem("h_lo_pool")
        q_zeroed = sem("q_zeroed")
        w_loaded = [sem(f"w_loaded{b}") for b in range(W_BUFS)]
        w_hi_done = sem("w_hi_done")
        w_lo_done = sem("w_lo_done")
        chain_done = sem("chain_done")
        proj_evicted = [sem("proj_evicted0"), sem("proj_evicted1")]
        scores_done = sem("scores_done")
        biased = sem("biased")
        maxed = sem("maxed")
        exped = sem("exped")
        pt_done = sem("pt_done")
        pt_evicted = sem("pt_evicted")
        pv_done = sem("pv_done")
        o_evicted = sem("o_evicted")
        vt_done = sem("vt_done")
        vt_evicted = sem("vt_evicted")
        xch_written = sem("xch_written")
        xch_read = sem("xch_read")
        comb = sem("comb")
        comb_exp = sem("comb_exp")
        comb_dve = sem("comb_dve")
        comb_pool = sem("comb_pool")
        z_exp = sem("z_exp")
        z_step = sem("z_step")
        ot_done = sem("ot_done")
        ot_evicted = sem("ot_evicted")
        o_hi_done = sem("o_hi_done")
        passed_pe = sem("passed_pe")
        passed_sp = sem("passed_sp")
        o_lo_done = sem("o_lo_done")
        x_stored = [sem(f"x_stored{k}") for k in range(KD)]

        gates_ab = sem("gates_ab")
        gate_step = sem("gate_step")
        gate_act = sem("gate_act")
        cum_done = sem("cum_done")
        rows_turned = sem("rows_turned")
        rows_out = sem("rows_out")
        head_set = sem("head_set")
        conv_step = sem("conv_step")
        silu_done = sem("silu_done")
        zsilu_done = sem("zsilu_done")
        sq_done = sem("sq_done")
        ss_done = sem("ss_done")
        rn_sqrt = sem("rn_sqrt")
        rn_done = sem("rn_done")
        nat_turned = sem("nat_turned")
        nat_out = sem("nat_out")
        vv_out = sem("vv_out")
        vb_out = sem("vb_out")
        kq_turned = sem("kq_turned")
        kq_out = sem("kq_out")
        gates_loaded = sem("gates_loaded")
        d_added = sem("d_added")
        d_exped = sem("d_exped")
        gk_done = sem("gk_done")
        qk_done = sem("qk_done")
        low_done = sem("low_done")
        qkm_done = sem("qkm_done")
        qkt_turned = sem("qkt_turned")
        qkt_out = sem("qkt_out")
        inv_zeroed = sem("inv_zeroed")
        blocks_stored = sem("blocks_stored")
        lanes_loaded = sem("lanes_loaded")
        sub_step = sem("sub_step")
        sub_done = sem("sub_done")
        inverses_stored = sem("inverses_stored")
        inv_loaded = sem("inv_loaded")
        inv_turned = sem("inv_turned")
        inv_t_out = sem("inv_t_out")
        low1_done = sem("low1_done")
        low2_done = sem("low2_done")
        x1_made = sem("x1_made")
        x1_out = sem("x1_out")
        vw_made = sem("vw_made")
        vw_out = sem("vw_out")
        x2_made = sem("x2_made")
        x2_out = sem("x2_out")
        fin_made = sem("fin_made")
        fin_out = sem("fin_out")
        kdec_done = sem("kdec_done")
        osq_step = sem("osq_step")
        orms_done = sem("orms_done")
        oscaled = sem("oscaled")
        oh_turned = sem("oh_turned")
        gated = sem("gated")
        heads_stored = sem("heads_stored")
        raw_padded = sem("raw_padded")
        qkt_back = sem("qkt_back")
        orms_inv = sem("orms_inv")
        passed_dve = sem("passed_dve")
        rows_copied_out = sem("rows_copied_out")
        conv_set = sem("conv_set")
        ks_made, qs_made, qs_out, r_out, vn_made, vn_out, ds_made, od_made, st_out, o_out = (
            [sem(f"{n}{d}") for d in range(DIRS)]
            for n in ("ks_made", "qs_made", "qs_out", "r_out", "vn_made", "vn_out", "ds_made", "od_made", "st_out", "o_out"))

        W_FREE = 2
        CH_FREE = 4
        EV_FREE = 1
        S_FREE = 2
        PT_FREE = 1
        PV_FREE = 2
        O_FREE = 1
        V_FREE = 2
        OT_FREE = 2
        XW_FREE = 1
        HEAD_FREE = 1

        consts = [(ident[:, :], d_ident), (ones[:, :], d_ones), (normw[:, :, :], norm_w),
                  (relb[:, :], rel_bias), (oneh, onehot), (outband[:, :], d_outband)]
        consts += [(conv_w[:, :, :, :], d_conv_w), (wab[:, :, :], d_wab), (a_log[:, :], d_a_log),
                   (dt_b[:, :], d_dt), (onorm[:, :], d_onorm), (tri[:, :, :], d_tri),
                   (masks[:, :, :], d_masks)]
        N_CONST = len(consts)

        def wait_alone(eng, passed, signal, value):
            eng.wait_ge(signal, value)
            eng.sem_inc(passed, 1)

        def combine_pool(pool, Pn):
            pool.wait_ge(comb, Pn * 8 + 6)
            o = o_sb[:, 1, :, 0:P].rearrange("p t (e d) -> p t e d", e=2)
            pool.tensor_tensor(o, o, wgt[:, 4, 1, :, :].unsqueeze(3).broadcast_to([P, QT, 2, HD]),
                               ALU.mult).then_inc(comb_pool, 1)


        def evicted_at_step(n_chain, per_step, kc=KD):
            return (3 * kc * (n_chain + 1) - 1) // per_step

        block = ctx.enter_context(nc.Block())

        @block.tensor
        def _(pe):
            pe.sem_inc(chain_done, CH_FREE)
            pe.sem_inc(pt_done, S_FREE)
            pe.sem_inc(pv_done, PV_FREE)

            def project(w0, par, first, count, kc=KD):
                per = 3 * kc
                for m in range(first, first + count):
                    i, r = divmod(m, 2 * per)
                    n, r = divmod(r, per)
                    k, part = divmod(r, 3)
                    b = (par + i) % 2
                    if m % (2 * per) == 0:
                        pe.wait_ge(w_hi_done, w0 + (i + 1 + W_FREE))
                        pe.wait_ge(w_lo_done, w0 + (i + 1 + W_FREE))
                    if r == 0:
                        pe.wait_ge(proj_evicted[n], w0 + (i + EV_FREE))
                    wt = (w_hi, w_hi, w_lo)[part][:, b, k * P:k * P + P]
                    ht = (h_hi, h_lo, h_hi)[part][:, k, HALF * n:HALF * n + HALF]
                    mm = pe.matmul(ps_proj[n][:, :], wt, ht, start=(r == 0), stop=(r == per - 1))
                    if r == per - 1:
                        mm.then_inc(chain_done, 1)

            def norm_sum(m):
                pe.wait_ge(summed, m * (KD - 1) + (KD - 1))
                for n in range(2):
                    pe.matmul(ps_proj[n][:, :], ones[:, :], sumsq[:, HALF * n:HALF * n + HALF],
                              start=True, stop=True).then_inc(sumsq_done, 1)

            def scores(g, slot, t, G):
                q0, k0, lo, hi = q_tile(g, t)
                pe.wait_ge(biased, G + 1)
                for e in range(2):
                    mm = pe.matmul(ps_s[t % 2][:, e * 256 + lo:e * 256 + hi],
                                   q_sb[:, slot, e, q0:q0 + P], k_sb[:, slot, k0 + lo:k0 + hi],
                                   start=True, stop=True)
                mm.then_inc(scores_done, 1)

            def turn_probs(g, t, G):
                pe.wait_ge(q_zeroed, 2)
                pe.wait_ge(exped, G + 1)
                pe.wait_ge(pt_evicted, G + PT_FREE)
                for c, (a, n, _) in enumerate(chunks(g, t)):
                    for e in range(2):
                        mm = pe.transpose(ps_pt[0:n, (2 * c + e) * P:(2 * c + e + 1) * P],
                                          s_sb[:, t % 2, e, a:a + n], ident[:, :])
                mm.then_inc(pt_done, 1)

            def weigh_values(g, t, G):
                pe.wait_ge(pt_evicted, G + (1 + PT_FREE))
                pe.wait_ge(o_evicted, G + O_FREE)
                cs = chunks(g, t)
                for e in range(2):
                    for c, (_, n, vt) in enumerate(cs):
                        mm = pe.matmul(ps_o[:, e * P:e * P + P],
                                       p_t[0:n, t % 2, (2 * c + e) * P:(2 * c + e + 1) * P],
                                       v_nat[0:n, vt, :], start=(c == 0), stop=(c == len(cs) - 1))
                mm.then_inc(pv_done, 1)

            def turn_values(g, slot, F):
                tiles = v_tiles(g)
                for f in range(0, len(tiles), 4):
                    wait_alone(pe, passed_pe, vt_evicted, F + (FILL0[slot] + f // 4 + 1))
                    bank = ps_v[(FILL0[slot] + f // 4) % 2]
                    for j, (c, n) in enumerate(tiles[f:f + 4]):
                        mm = pe.transpose(bank[0:n, j * P:j * P + P], v_ch[:, c:c + n], ident[:, :])
                    mm.then_inc(vt_done, 1)

            def unit(slot, Pn, own_v, w0, par, per_slot):
                g = SLOTS[slot]
                G0 = Pn * 24 + 8 * slot
                pe.wait_ge(proj_evicted[0], own_v + (1 + EV_FREE))
                pe.wait_ge(proj_evicted[1], own_v + (1 + EV_FREE))
                if slot == 0:
                    pe.wait_ge(ot_evicted, Pn * 2 + OT_FREE)
                scores(g, slot, 0, G0)
                turn_values(g, slot, Pn * 8)
                for t in range(QT):
                    if t + 1 < QT:
                        scores(g, slot, t + 1, G0 + (t + 1))
                    project(w0, par, 3 * per_slot * t, per_slot)
                    turn_probs(g, t, G0 + t)
                    project(w0, par, 3 * per_slot * t + per_slot, per_slot)
                    weigh_values(g, t, G0 + t)
                    project(w0, par, 3 * per_slot * t + 2 * per_slot, per_slot)

            def pair(s, p, last):
                Pn = s * PAIRS + p
                W = s * STREAM + p * 10
                unit(0, Pn, W + 2, W + 3, 1, 6)
                unit(1, Pn, W + 5, W + 6, 0, 6)
                unit(2, Pn, W + 8, W + 9, 1, 2 if last else 6)
                if not last:
                    project(W + 9, 1, 144, 48)
                pe.wait_ge(comb, Pn * 8 + 8)
                pe.wait_ge(vt_evicted, Pn * 8 + (8 + V_FREE))
                for n in range(2):
                    for j in range(4):
                        mm = pe.transpose(ps_v[n][:, j * P:j * P + P], o_sb[:, 0, 4 * n + j, 0:P],
                                          ident[:, :])
                    mm.then_inc(ot_done, 1)

            def project_first(w, m):
                pe.wait_ge(w_hi_done, w + (1 + W_FREE))
                pe.wait_ge(w_lo_done, w + (1 + W_FREE))
                for n in range(2):
                    pe.wait_ge(proj_evicted[n], w + EV_FREE)
                for k in range(KD):
                    pe.wait_ge(h_lo_pool if k % 2 else h_lo_dve, m * (KD // 2) + (k // 2 + 1))
                    for n in range(2):
                        for part in range(3):
                            mm = pe.matmul(ps_proj[n][:, :],
                                           (w_hi, w_hi, w_lo)[part][:, 0, k * P:k * P + P],
                                           (h_hi, h_lo, h_hi)[part][:, k, HALF * n:HALF * n + HALF],
                                           start=(k == 0 and part == 0), stop=(k == KD - 1 and part == 2))
                        if k == KD - 1:
                            mm.then_inc(chain_done, 1)

            def gate_products(s):
                pe.wait_ge(h_scaled, s * (3 * KD) + 2 * KD)
                for c in range(NC):
                    for k in range(KD):
                        mm = pe.matmul(psum[2][:, c * 4 * DH:(c + 1) * 4 * DH],
                                       x_sb[:, k, c * P:(c + 1) * P], wab[:, k, :],
                                       start=(k == 0), stop=(k == KD - 1))
                mm.then_inc(gates_ab, 1)

            def gate_sums(s):
                pe.wait_ge(gate_step, s * G_STEPS + 10)
                half = DH * NC
                for d in range(DIRS):
                    pe.matmul(psum[3][:, d * half:(d + 1) * half], tri[:, d, :],
                              gt[:, 8, d * half:(d + 1) * half], start=True, stop=True)
                pe.matmul(psum[3][:, P:2 * P], ones[:, :], gt[:, 8, :],
                          start=True, stop=True).then_inc(cum_done, 1)
                pe.wait_ge(gate_step, s * G_STEPS + 15)
                pe.transpose(psum[4][:, 0:P], gates[:, 0:2, :, :].rearrange("p d h n -> p (d h n)"),
                             ident[:, :]).then_inc(rows_turned, 1)

            def front(H, Wn):
                for i in range(2):
                    pe.wait_ge(sq_done, H * 2 + (i + 1))
                    for c in range(NC):
                        mm = pe.matmul(psum[6 + i][:, c:c + 1],
                                       sq_h[:, i, c * P:(c + 1) * P], ones[:, 0:1],
                                       start=True, stop=True)
                    mm.then_inc(ss_done, 1)
                for n in range(2):
                    pe.wait_ge(proj_evicted[n], Wn + EV_FREE)
                for i in range(3):
                    pe.wait_ge(silu_done, H * 3 + (i + 1))
                    for half in range(2):
                        for c in range(4):
                            t = (4 * half + c) * P
                            mm = pe.transpose(psum[(2, 4, 0)[i] + half][:, c * P:(c + 1) * P],
                                              cv[i][:, t:t + P], ident[:, :])
                        mm.then_inc(nat_turned, 1)
                for i in range(2):
                    for half in range(2):
                        pe.wait_ge(nat_out, H * 4 + (2 * i + half + 1))
                        for c in range(4):
                            mm = pe.transpose(psum[2 + 2 * i + half][:, c * P:(c + 1) * P],
                                              nat[:, i, 4 * half + c, :], ident[:, :])
                        mm.then_inc(kq_turned, 1)
                pe.wait_ge(kq_out, H * 4 + 4)
                for j in range(4):
                    bank = psum[(2, 3, 6, 7)[j]]
                    for e in range(2):
                        mm = pe.matmul(bank[:, 2 * P * e:2 * P * (e + 1)], kq[:, 2 * j + e, 0, :],
                                       kq[:, 2 * j + e, :, :].rearrange("p a c -> p (a c)"),
                                       start=True, stop=True)
                    mm.then_inc(gk_done, 1)
                for half in range(2):
                    for c in range(4):
                        mm = pe.matmul(psum[4 + half][:, c * P:(c + 1) * P], kq[:, 4 * half + c, 1, :],
                                       kq[:, 4 * half + c, 0, :], start=True, stop=True)
                    mm.then_inc(qk_done, 1)

            def turn_attention(H):
                for half in range(2):
                    pe.wait_ge(qkm_done, H * 2 + (half + 1))
                    for c in range(4):
                        mm = pe.transpose(psum[4 + half][:, c * P:(c + 1) * P],
                                          qkm[:, 4 * half + c, :], ident[:, :])
                    mm.then_inc(qkt_turned, 1)

            def turn_outputs(H):
                pe.wait_ge(oscaled, H + 1)
                for half in range(2):
                    for c in range(4):
                        mm = pe.transpose(psum[2 + half][:, c * P:(c + 1) * P],
                                          o_dir[:, 0, 4 * half + c, :], ident[:, :])
                    mm.then_inc(oh_turned, 1)

            def fill_front(H, Wn, tail, fill):
                if fill:
                    pe.wait_ge(vv_out, H * 2 + 2)
                    pe.wait_ge(vb_out, H * 2 + 2)
                    project(Wn, 0, 0, 40)
                turn_attention(H)
                if fill:
                    project(Wn, 0, 40, 8)
                if tail is not None:
                    turn_outputs(tail)
                if fill:
                    project(Wn, 0, 48, 96)

            def head(H, Wn, more):
                pe.wait_ge(inv_loaded, H * 64 + 64)
                pe.wait_ge(qkt_out, H * 2 + 2)
                pe.wait_ge(gated, H * 2 + HEAD_FREE)
                for g in range(4):
                    if g > 1:
                        pe.wait_ge(inv_t_out, H * 4 + (g - 1))
                    for j in range(4):
                        mm = pe.transpose(psum[6 + g % 2][:, j * P:(j + 1) * P],
                                          inv[:, 4 * g + j, :], ident[:, :])
                    mm.then_inc(inv_turned, 1)

                def first_x(g):
                    pe.wait_ge(inv_t_out, H * 4 + (g + 1))
                    if g > 1:
                        pe.wait_ge(x1_out, H * 4 + (g - 1))
                    for j in range(4):
                        mm = pe.matmul(psum[2 + g % 2][:, j * P:(j + 1) * P], low1[:, 4 * g + j, :],
                                       inv_t[:, 4 * g + j, :], start=True, stop=True)
                    mm.then_inc(x1_made, 1)

                def first_vw(g):
                    pe.wait_ge(x1_out, H * 4 + (g + 1))
                    pe.wait_ge(inv_t_out, H * 4 + 4)
                    if g > 1:
                        pe.wait_ge(vw_out, H * 4 + (g - 1))
                    for j in range(4):
                        u = 4 * g + j
                        pe.matmul(psum[4 + g % 2][:, j * P:(j + 1) * P], inv[:, u, :], xm[:, u, :],
                                  start=True, stop=True)
                        mm = pe.matmul(psum[6 + g % 2][:, j * P:(j + 1) * P], xm[:, u, :], inv[:, u, :],
                                       start=True, stop=True)
                    mm.then_inc(vw_made, 1)

                def second_x(g):
                    if g > 1:
                        pe.wait_ge(x2_out, H * 4 + (g - 1))
                    for j in range(4):
                        mm = pe.matmul(psum[2 + g % 2][:, j * P:(j + 1) * P], low[:, 4 * g + j, :],
                                       inv_t[:, 4 * g + j, :], start=True, stop=True)
                    mm.then_inc(x2_made, 1)

                def second_f(g):
                    pe.wait_ge(x2_out, H * 4 + (g + 1))
                    if g > 1:
                        pe.wait_ge(fin_out, H * 4 + (g - 1))
                    for j in range(4):
                        u = 4 * g + j
                        a, b = (xm, inv) if j % 2 else (inv, xm)
                        mm = pe.matmul(psum[4 + g % 2][:, j * P:(j + 1) * P], a[:, u, :], b[:, u, :],
                                       start=True, stop=True)
                    mm.then_inc(fin_made, 1)

                pe.wait_ge(low1_done, H + 1)
                first_x(0)
                first_x(1)
                for g in range(4):
                    first_vw(g)
                    if g < 2:
                        first_x(g + 2)
                pe.wait_ge(low2_done, H + 1)
                pe.wait_ge(vw_out, H * 4 + 4)
                second_x(0)
                second_x(1)
                for g in range(4):
                    second_f(g)
                    if g < 2:
                        second_x(g + 2)

                pe.wait_ge(fin_out, H * 4 + 4)
                pe.wait_ge(vv_out, H * 2 + 2)
                pe.wait_ge(vb_out, H * 2 + 2)
                pe.wait_ge(kdec_done, H * 2 + 2)
                for i in range(NC):
                    ends = (i, NC - 1 - i)
                    if i:
                        for d in range(DIRS):
                            pe.wait_ge(st_out[d], H * (NC - 1) + i)
                            pe.matmul(psum[6 + d][:, 0:P], kq[:, ends[d], 0, :], state[:, d, :],
                                      start=True, stop=True).then_inc(ks_made[d], 1)
                        for d in range(DIRS):
                            pe.matmul(psum[4 + d][:, 0:P], kq[:, ends[d], 1, :], state[:, d, :],
                                      start=True, stop=True).then_inc(qs_made[d], 1)
                    if more:
                        project(Wn, 0, 144 + 6 * i, 2)
                    for d in range(DIRS):
                        if i:
                            pe.wait_ge(qs_out[d], H * (NC - 1) + i)
                            pe.wait_ge(r_out[d], H * (NC - 1) + i)
                        pe.matmul(psum[4 + d][:, 0:P], inv_t[:, 2 * ends[d] + d, :],
                                  rhs[:, d, :] if i else vv[:, d, ends[d], :],
                                  start=True, stop=True).then_inc(vn_made[d], 1)
                    if more:
                        project(Wn, 0, 146 + 6 * i, 2)
                    for d in range(DIRS):
                        pe.wait_ge(vn_out[d], H * NC + (i + 1))
                        if i < NC - 1:
                            pe.matmul(psum[6 + d][:, P:2 * P], kdec[:, d, ends[d], :], v_new[:, d, :],
                                      start=True, stop=True).then_inc(ds_made[d], 1)
                    for d in range(DIRS):
                        if i:
                            pe.wait_ge(o_out[d], H * NC + i)
                        pe.matmul(psum[2 + d][:, 0:P], qkt[:, 2 * ends[d] + d, :], v_new[:, d, :],
                                  start=True, stop=True).then_inc(od_made[d], 1)
                    if more:
                        project(Wn, 0, 148 + 6 * i, 2)
                for d in range(DIRS):
                    pe.wait_ge(o_out[d], H * NC + NC)
                if more:
                    front(H + 1, Wn + 4)
                    fill_front(H + 1, Wn + 4, H, more > 1)
                else:
                    turn_outputs(H)

            def layer_b(s):
                W = s * STREAM + B0
                norm_sum(s * 3 + 1)
                project_first(W, s * 3 + 1)
                gate_products(s)
                project(W, 0, 48, 24)
                gate_sums(s)
                project(W, 0, 72, 120)
                front(s * DH, W + 4)
                fill_front(s * DH, W + 4, None, True)
                with pe.Fori(0, DH - 2) as h:
                    head(s * DH + h, h * 4 + s * STREAM + (B0 + 4), 2)
                head(s * DH + (DH - 2), s * STREAM + (B0 + B_TILES - 4), 1)
                head(s * DH + (DH - 1), s * STREAM + (B0 + B_TILES), 0)
                project_first(s * STREAM + (B0 + B_TILES), s * 3 + 2)
                project(s * STREAM + (B0 + B_TILES), 0, 6 * KD, (O_TILES - 1) * 6 * KD)
                norm_sum(s * 3 + 2)

            pe.wait_ge(const_loaded, 16 * N_CONST)
            for g in range(NG):
                pe.matmul(psum[g][0:HEADS, 0:REL], relb[:, g * HEADS:(g + 1) * HEADS],
                          oneh[:, g, :], start=True, stop=True).then_inc(rows_done, 1)
            pe.wait_ge(rows_copied, NG)

            pe.wait_ge(q_zeroed, 2)

            with pe.Fori(0, SEQS) as s:
                norm_sum(s * 3)
                pe.wait_ge(q_zeroed, s * 2 + 2)
                project_first(s * STREAM, s * 3)
                project(s * STREAM, 0, 48, 96)
                with pe.Fori(0, PAIRS - 1) as p:
                    pair(s, p, False)
                pair(s, PAIRS - 1, True)
                wait_alone(pe, passed_pe, o_hi_done, s * 4 + 4)
                wait_alone(pe, passed_pe, o_lo_done, s * 4 + 4)
                with pe.Fori(0, O_TILES // 2) as i:
                    project(s * STREAM + i * 2 + A_TILES, 0, 0, 4 * 3 * KC_A, kc=KC_A)
                layer_b(s)

        @block.vector
        def _(dve):
            for n in range(2):
                dve.sem_inc(proj_evicted[n], EV_FREE)
            dve.sem_inc(biased, S_FREE)
            dve.sem_inc(o_evicted, O_FREE)
            dve.sem_inc(ot_evicted, OT_FREE)
            dve.sem_inc(gated, HEAD_FREE)

            def add_square(k, m):
                dve.wait_ge(squared, m * KD + (k + 1))
                if k > 1:
                    dve.wait_ge(summed, m * (KD - 1) + (k - 1))
                dve.tensor_tensor(sumsq, sumsq, sq[:, k % 2, :], ALU.add).then_inc(summed, 1)

            def split_even(m, k):
                dve.wait_ge(h_hi_done, m * KD + (k + 1))
                dve.tensor_tensor(h_lo[:, k, :], x_sb[:, k, :], h_hi[:, k, :].bitcast(F32),
                                  ALU.subtract).then_inc(h_lo_dve, 1)

            def scale(m, layer, stored=None, parts=False):
                for n in range(2):
                    dve.wait_ge(rms_done, m * 2 + (n + 1))
                    half = slice(HALF * n, HALF * n + HALF)
                    dve.reciprocal(rstd[:, half], rstd[:, half]).then_inc(rstd_done, 1)
                dve.wait_ge(rstd_done, m * 2 + 2)
                for k in range(KD):
                    if stored is not None:
                        dve.wait_ge(x_stored[k], stored * 32 + 16)
                    dve.scalar_tensor_tensor(out=x_sb[:, k, :], in0=x_sb[:, k, :],
                                             scalar=normw[:, layer, k:k + 1], in1=rstd,
                                             op0=ALU.mult, op1=ALU.mult).then_inc(h_scaled, 1)
                    if parts and k % 2:
                        split_even(m, k - 1)

            def take_out(kind, n, g, slot, w):
                if kind == "q":
                    dve.wait_ge(chain_done, w * 2 + (n + 1 + CH_FREE))
                    for e in range(2):
                        r = slice(HD * e, HD * e + HD)
                        out, src = in_group_order(q_sb[r, slot, e, :], ps_proj[n][r, :], g, n)
                        mv = dve.tensor_copy(out, src)
                    mv.then_inc(proj_evicted[n], 1)
                elif kind == "z":
                    half = slice(HALF * n, HALF * n + HALF)
                    c = w_z[0]
                    dve.wait_ge(z_exp, c + (n + 1))
                    dve.tensor_scalar(zs[:, half], zs[:, half], 1.0, None,
                                      ALU.add).then_inc(z_step, 1)
                    dve.wait_ge(z_step, c * 2 + (2 * n + 1))
                    dve.reciprocal(zs[:, half], zs[:, half]).then_inc(z_step, 1)
                    dve.wait_ge(z_step, c * 2 + (2 * n + 2))
                    dve.tensor_tensor(zs[:, half], ps_proj[n][:, :], zs[:, half],
                                      ALU.mult).then_inc(proj_evicted[n], 1)

            w_z = [None]

            def soften(g, slot, t, G, Pn, p):
                _, _, lo, hi = q_tile(g, t)
                dve.wait_ge(scores_done, G + 1)
                dve.wait_ge(pt_done, G + 1)
                bias = bias2[:, bass.ds(p * 2, 2), :] if g == 2 else \
                    bias01[g][:, bass.ds(p * 2, 2), lo:hi]
                dve.scalar_tensor_tensor(
                    out=s_sb[:, t % 2, :, lo:hi],
                    in0=ps_s[t % 2].rearrange("p (e k) -> p e k", e=2)[:, :, lo:hi],
                    scalar=SCALE, in1=bias, op0=ALU.mult, op1=ALU.add).then_inc(biased, 1)
                dve.wait_ge(biased, G + (1 + S_FREE))
                dve.tensor_reduce(o_sb[:, O_OF[slot], t, P:P + 2], s_sb[:, t % 2, :, lo:hi], AX.X,
                                  ALU.max, negate=True).then_inc(maxed, 1)

            def take_output(slot, t, G):
                dve.wait_ge(pv_done, G + (1 + PV_FREE))
                dve.tensor_copy(
                    o_sb[:, O_OF[slot], t, 0:P].rearrange("p (e d) -> p e d", e=2),
                    bass.AP(ps_o, 0, [[HALF, P], [P + HD, 2], [1, HD]])).then_inc(o_evicted, 1)

            def unit(s, slot, Pn, p, w0, kinds, gs, slots, per_step):
                g = SLOTS[slot]
                G0 = Pn * 24 + 8 * slot
                if slot == 0:
                    dve.wait_ge(xch_written, Pn * 48 + XW_FREE)
                soften(g, slot, 0, G0, Pn, p)
                for t in range(QT):
                    if t + 1 < QT:
                        soften(g, slot, t + 1, G0 + (t + 1), Pn, p)
                    take_output(slot, t, G0 + t)
                    for c in range(2 * len(kinds)):
                        if evicted_at_step(c, per_step) == t and kinds[c // 2] in "qz":
                            take_out(kinds[c // 2], c % 2, gs, slots, w0 + c // 2)

            def combine(Pn, s):
                stats = o_sb[:, 0:3, :, P:P + 2]
                low, e, t = wgt[:, 0, 0, :, :], wgt[:, 1, :, :, :], wgt[:, 2, :, :, :]
                total, w = wgt[:, 3, 0, :, :], wgt[:, 4, :, :, :]
                dve.wait_ge(xch_read, Pn * 32 + 32)
                dve.wait_ge(maxed, Pn * 24 + 24)
                dve.wait_ge(exped, Pn * 24 + 24)
                dve.tensor_reduce(low, stats.rearrange("p g t e -> p t e g"), AX.X,
                                  ALU.min).then_inc(comb, 1)
                dve.wait_ge(comb, Pn * 8 + 1)
                dve.tensor_tensor(e, wgt[:, 0, 0:1, :, :].broadcast_to([P, 3, QT, 2]), stats,
                                  ALU.subtract).then_inc(comb, 1)
                dve.wait_ge(comb_exp, Pn + 1)
                dve.tensor_tensor(t, e, o_sb[:, 0:3, :, P + 2:P + 4], ALU.mult).then_inc(comb, 1)
                dve.wait_ge(comb, Pn * 8 + 3)
                dve.tensor_reduce(total, t.rearrange("p g t e -> p t e g"), AX.X,
                                  ALU.add).then_inc(comb, 1)
                dve.wait_ge(comb, Pn * 8 + 4)
                dve.reciprocal(total, total).then_inc(comb, 1)
                dve.wait_ge(comb, Pn * 8 + 5)
                dve.tensor_tensor(w, e, wgt[:, 3, 0:1, :, :].broadcast_to([P, 3, QT, 2]),
                                  ALU.mult).then_inc(comb, 1)
                dve.wait_ge(comb, Pn * 8 + 6)
                for g in (0, 2):
                    o = o_sb[:, g, :, 0:P].rearrange("p t (e d) -> p t e d", e=2)
                    mv = dve.tensor_tensor(o, o, wgt[:, 4, g, :, :].unsqueeze(3).broadcast_to(
                        [P, QT, 2, HD]), ALU.mult)
                    mv.then_inc(comb_dve, 1)
                dve.wait_ge(comb_dve, Pn * 2 + 2)
                dve.tensor_tensor(o_sb[:, 0, :, 0:P], o_sb[:, 0, :, 0:P], o_sb[:, 2, :, 0:P],
                                  ALU.add).then_inc(comb, 1)
                dve.wait_ge(comb, Pn * 8 + 7)
                dve.wait_ge(comb_pool, Pn + 1)
                dve.tensor_tensor(o_sb[:, 0, :, 0:P], o_sb[:, 0, :, 0:P], o_sb[:, 1, :, 0:P],
                                  ALU.add).then_inc(comb, 1)

            def gate(Pn, p, s, w):
                for n in range(2):
                    dve.wait_ge(ot_done, Pn * 2 + (n + 1))
                    dve.wait_ge(proj_evicted[n], w + (1 + EV_FREE))
                    dve.tensor_tensor(
                        o_all[:, bass.ds(p, 1), HALF * n:HALF * n + HALF].rearrange("p a t -> p (a t)"),
                        ps_v[n][:, :], zs[:, HALF * n:HALF * n + HALF], ALU.mult).then_inc(ot_evicted, 1)

            def pair(s, p, last):
                Pn = s * PAIRS + p
                W = s * STREAM + p * 10
                w_z[0] = Pn * 2
                unit(s, 0, Pn, p, W + 3, "qkv", SLOTS[1], 1, 18)
                unit(s, 1, Pn, p, W + 6, "qkv", SLOTS[2], 2, 18)
                if last:
                    unit(s, 2, Pn, p, W + 9, "z", None, None, 6)
                else:
                    unit(s, 2, Pn, p, W + 9, "zqk", SLOTS[0], 0, 18)
                combine(Pn, s)
                gate(Pn, p, s, W + 9)

            def add_input(q, m, w0):
                for k in range(O_TILES):
                    dve.wait_ge(x_loaded[k], q * 16 + 16)
                    for n in range(2):
                        half = slice(HALF * n, HALF * n + HALF)
                        dve.wait_ge(chain_done, w0 * 2 + (2 * k + n + 1 + CH_FREE))
                        dve.tensor_tensor(x_sb[:, k, half], ps_proj[n][:, :],
                                          x_sb[:, k, half], ALU.add).then_inc(proj_evicted[n], 1)
                    if k > 1:
                        add_square(k - 1, m)
                add_square(KD - 1, m)

            def gate_values(s):
                G = s * G_STEPS
                A = s * G_ACTS
                ab = psum[2][:, 0:NC * 4 * DH].rearrange("p (n c) -> p c n", c=4 * DH)

                def by_gate(v):
                    return v.rearrange("p (c n) -> p c n", n=NC)

                def kind(i, d=None):
                    k = gates[:, 2 * i:2 * i + 2] if d is None else gates[:, 2 * i + d:2 * i + d + 1]
                    return k.rearrange("p d h n -> p (d h n)")

                x, ax, e, eb, A_, u, ln, den, g = (gt[:, i, :] for i in range(9))
                A_ = A_[:, 0:DIRS * DH]
                dve.wait_ge(gates_ab, s + 1)
                dve.tensor_tensor(by_gate(x), ab[:, 0:DIRS * DH, :],
                                  dt_b[:, :].unsqueeze(2).broadcast_to([P, DIRS * DH, NC]),
                                  ALU.add).then_inc(gate_step, 1)
                dve.wait_ge(gate_step, G + 1)
                dve.scalar_tensor_tensor(out=ax, in0=x, scalar=-1.0, in1=x, op0=ALU.mult,
                                         op1=ALU.max).then_inc(gate_step, 1)
                dve.wait_ge(gate_act, A + 1)
                dve.tensor_scalar(u, e, 1.0, None, ALU.add).then_inc(gate_step, 1)
                dve.wait_ge(gate_step, G + 3)
                dve.tensor_scalar(den, u, -1.0, TINY, ALU.add, ALU.add).then_inc(gate_step, 1)
                dve.wait_ge(gate_step, G + 4)
                dve.reciprocal(den, den).then_inc(gate_step, 1)
                dve.wait_ge(gate_step, G + 5)
                dve.wait_ge(gate_act, A + 4)
                dve.scalar_tensor_tensor(out=ln, in0=ln, scalar=TINY, in1=den, op0=ALU.add,
                                         op1=ALU.mult).then_inc(gate_step, 1)
                dve.wait_ge(gate_step, G + 6)
                dve.tensor_tensor(ln, ln, e, ALU.mult).then_inc(gate_step, 1)
                dve.wait_ge(gate_step, G + 7)
                dve.scalar_tensor_tensor(out=ax, in0=x, scalar=0.0, in1=ln, op0=ALU.max,
                                         op1=ALU.add).then_inc(gate_step, 1)
                dve.tensor_scalar(A_, A_, -1.0, None, ALU.mult).then_inc(gate_step, 1)
                dve.wait_ge(gate_step, G + 9)
                dve.tensor_tensor(by_gate(g), by_gate(ax),
                                  A_.unsqueeze(2).broadcast_to([P, DIRS * DH, NC]),
                                  ALU.mult).then_inc(gate_step, 1)
                dve.tensor_scalar(eb, eb, 1.0, None, ALU.add).then_inc(gate_step, 1)
                dve.wait_ge(gate_step, G + 11)
                dve.reciprocal(kind(BETA), eb).then_inc(gate_step, 1)
                dve.wait_ge(gate_step, G + 12)
                dve.tensor_scalar(kind(NBETA), kind(BETA), -1.0, None, ALU.mult).then_inc(gate_step, 1)
                half = DH * NC
                dve.wait_ge(gate_act, A + 7)
                dve.tensor_copy(kind(GSGN, 0), x[:, 0:half]).then_inc(gate_step, 1)
                dve.tensor_scalar(kind(GSGN, 1), x[:, half:], -1.0, None, ALU.mult).then_inc(gate_step, 1)
                dve.tensor_tensor(ax, psum[3][:, P:2 * P], x, ALU.subtract).then_inc(gate_step, 1)
                dve.wait_ge(gate_step, G + 13)
                dve.tensor_tensor(kind(COEF, 0), kind(NBETA, 0), kind(EG, 0), ALU.mult).then_inc(gate_step, 1)
                dve.tensor_scalar(kind(COEF, 1), kind(EG, 1), -1.0, None, ALU.mult).then_inc(gate_step, 1)

            def take_conv_weights(h, H):
                dve.tensor_copy(conv_h, conv_w[:, :, bass.ds(h, 1), :].rearrange("p i a t -> p i (a t)")).then_inc(conv_set, 1)
                dve.wait_ge(conv_set, H + 1)

            def convolve(H, first, count):
                for m in range(first, first + count):
                    i, t = divmod(m, CONV_K)
                    if t == 0:
                        dve.tensor_scalar(cv[i], raw[:, i, 0:S], conv_h[:, i, 0:1], None,
                                          ALU.mult).then_inc(conv_step, 1)
                    else:
                        dve.wait_ge(conv_step, H * (3 * CONV_K) + m)
                        dve.scalar_tensor_tensor(out=cv[i], in0=raw[:, i, t:t + S],
                                                 scalar=conv_h[:, i, t:t + 1], in1=cv[i],
                                                 op0=ALU.mult, op1=ALU.add).then_inc(conv_step, 1)

            def front(h, H, tail):
                by_kind = gate_h.rearrange("p k d n -> p (k d) n")
                dve.tensor_copy(by_kind, gates[:, :, bass.ds(h, 1), :].rearrange("p k a n -> p k (a n)")).then_inc(head_set, 1)
                dve.wait_ge(head_set, H + 1)
                dve.wait_ge(rn_sqrt, H * 2 + 2)
                dve.reciprocal(rnorm, rnorm).then_inc(rn_done, 1)
                dve.wait_ge(rn_done, H + 1)
                for i in range(2):
                    for half in range(2):
                        c = slice(4 * half, 4 * half + 4)
                        dve.wait_ge(nat_turned, H * 6 + (2 * i + 2))
                        dve.tensor_tensor(nat[:, i, c, :],
                                          psum[2 + 2 * i + half].rearrange("p (c t) -> p c t", c=4),
                                          rnorm[:, i, c].unsqueeze(2).broadcast_to([P, 4, P]),
                                          ALU.mult).then_inc(nat_out, 1)
                for half in range(2):
                    c = slice(4 * half, 4 * half + 4)
                    dve.wait_ge(vb_out, H * 2 + (half + 1))
                    dve.tensor_tensor(vv[:, 0, c, :], psum[half].rearrange("p (c t) -> p c t", c=4),
                                      gate_h[:, BETA, 0, c].unsqueeze(2).broadcast_to([P, 4, P]),
                                      ALU.mult).then_inc(vv_out, 1)
                if tail is not None:
                    sum_outputs(tail)
                for j in range(4):
                    bank = psum[(2, 3, 6, 7)[j]].rearrange("p (e a t) -> p e a t", e=2, a=2)
                    dve.wait_ge(gk_done, H * 4 + (j + 1))
                    dve.wait_ge(d_exped, H * 4 + (j + 1))
                    for e in range(2):
                        for d in range(DIRS):
                            c = 2 * j + e
                            mv = dve.scalar_tensor_tensor(
                                out=low[:, 2 * c + d, :], in0=bank[:, e, 0, :],
                                scalar=gate_h[:, NBETA, d, c:c + 1], in1=decay[:, 2 * c + d, :],
                                op0=ALU.mult, op1=ALU.mult)
                    mv.then_inc(low_done, 1)
                    units = slice(4 * j, 4 * j + 4)
                    back = [v[:, units, :].rearrange("p (e d) t -> p e d t", d=2)[:, :, 1, :]
                            for v in (qkt, decay)]
                    dve.tensor_tensor(back[0], bank[:, :, 1, :], back[1], ALU.mult).then_inc(qkt_back, 1)
                for half in range(2):
                    dve.wait_ge(qk_done, H * 2 + (half + 1))
                    fwd = decay.rearrange("p (c d) t -> p c d t", d=2)[:, 4 * half:4 * half + 4, 0, :]
                    dve.tensor_tensor(qkm[:, 4 * half:4 * half + 4, :],
                                      psum[4 + half].rearrange("p (c t) -> p c t", c=4), fwd,
                                      ALU.mult).then_inc(qkm_done, 1)
                dve.wait_ge(qkm_done, H * 2 + 2)
                dve.wait_ge(qkt_back, H * 4 + 4)
                dve.memset(inv.rearrange("p u t -> p (u t)"), 0.0).then_inc(inv_zeroed, 1)
                if tail is not None:
                    finish(tail)
                dve.wait_ge(lanes_loaded, H * 16 + 16)
                steps = 0
                for j in range(1, BLK - 1):
                    below = slice(j + 1, BLK)
                    shape = [LANES, BLK - 1 - j, j]
                    if steps:
                        dve.wait_ge(sub_step, H * SUB_STEPS + steps)
                    dve.tensor_tensor(ltmp[0:LANES, below, 0:j],
                                      lanes[0:LANES, below, j:j + 1].broadcast_to(shape),
                                      lanes[0:LANES, j:j + 1, 0:j].broadcast_to(shape),
                                      ALU.mult).then_inc(sub_step, 1)
                    dve.wait_ge(sub_step, H * SUB_STEPS + (steps + 1))
                    dve.tensor_tensor(lanes[0:LANES, below, 0:j], lanes[0:LANES, below, 0:j],
                                      ltmp[0:LANES, below, 0:j], ALU.add).then_inc(sub_step, 1)
                    steps += 2
                assert steps == SUB_STEPS
                dve.wait_ge(sub_step, H * SUB_STEPS + steps)
                flat = lanes.rearrange("p i j -> p (i j)")
                dve.memset(flat[0:LANES, 0:BLK * BLK:BLK + 1], 1.0).then_inc(sub_done, 1)
                if tail is not None:
                    gate_outputs(tail)

            def head(h, H, Wn, more):
                if more:
                    take_conv_weights(h + 1, H + 1)
                    for n in range(2):
                        dve.wait_ge(proj_evicted[n], Wn + (3 + EV_FREE))
                    dve.wait_ge(kdec_done, H * 2 + 2)
                    convolve(H + 1, 0, 2 * CONV_K)
                for g in range(4):
                    u = slice(4 * g, 4 * g + 4)
                    dve.wait_ge(vw_made, H * 4 + (g + 1))
                    dve.tensor_tensor(inv_t[:, u, :], inv_t[:, u, :],
                                      psum[4 + g % 2].rearrange("p (j t) -> p j t", j=4), ALU.add)
                    dve.tensor_tensor(inv[:, u, :], inv[:, u, :],
                                      psum[6 + g % 2].rearrange("p (j t) -> p j t", j=4),
                                      ALU.add).then_inc(vw_out, 1)
                dve.wait_ge(vw_out, H * 4 + 4)
                for g in range(4):
                    dve.wait_ge(fin_made, H * 4 + (g + 1))
                    for d, m in enumerate((inv_t, inv)):
                        mine, old = (v[:, 4 * g:4 * g + 4, :].rearrange("p (e d) t -> p e d t", d=2)[:, :, d, :]
                                     for v in (inv_t, m))
                        mv = dve.tensor_tensor(
                            mine, old,
                            psum[4 + g % 2].rearrange("p (e d t) -> p e d t", e=2, d=2)[:, :, d, :],
                            ALU.add)
                    mv.then_inc(fin_out, 1)
                for i in range(NC):
                    ends = (i, NC - 1 - i)
                    if i:
                        for d in range(DIRS):
                            dve.wait_ge(ks_made[d], H * (NC - 1) + i)
                            dve.scalar_tensor_tensor(
                                out=rhs[:, d, :], in0=psum[6 + d][:, 0:P],
                                scalar=gate_h[:, COEF, d, ends[d]:ends[d] + 1],
                                in1=vv[:, d, ends[d], :], op0=ALU.mult,
                                op1=ALU.add).then_inc(r_out[d], 1)
                    if more and 0 < i <= CONV_K:
                        convolve(H + 1, 2 * CONV_K + (i - 1), 1)
                    for d in range(DIRS):
                        if i == NC - 1:
                            break
                        dve.wait_ge(ds_made[d], H * (NC - 1) + (i + 1))
                        if i == 0:
                            dve.tensor_copy(state[:, d, :], psum[6 + d][:, P:2 * P]).then_inc(st_out[d], 1)
                        else:
                            dve.wait_ge(st_out[d], H * (NC - 1) + i)
                            dve.scalar_tensor_tensor(
                                out=state[:, d, :], in0=state[:, d, :],
                                scalar=gate_h[:, EGL, d, ends[d]:ends[d] + 1],
                                in1=psum[6 + d][:, P:2 * P], op0=ALU.mult,
                                op1=ALU.add).then_inc(st_out[d], 1)
                    for d in range(DIRS):
                        dve.wait_ge(od_made[d], H * NC + (i + 1))
                        if i == 0:
                            mv = dve.tensor_copy(o_dir[:, d, ends[d], :], psum[2 + d][:, 0:P])
                        else:
                            dve.wait_ge(qs_out[d], H * (NC - 1) + i)
                            mv = dve.tensor_tensor(o_dir[:, d, ends[d], :], o_dir[:, d, ends[d], :],
                                                   psum[2 + d][:, 0:P], ALU.add)
                        mv.then_inc(o_out[d], 1)
                if more:
                    front(h + 1, H + 1, H)
                else:
                    sum_outputs(H)
                    finish(H)
                    gate_outputs(H)

            def sum_outputs(H):
                for d in range(DIRS):
                    dve.wait_ge(o_out[d], H * NC + NC)
                dve.tensor_tensor(o_dir[:, 0, :, :], o_dir[:, 0, :, :], o_dir[:, 1, :, :],
                                  ALU.add).then_inc(osq_step, 1)
                dve.wait_ge(osq_step, H * 3 + 1)
                dve.tensor_tensor(o_dir[:, 1, :, :], o_dir[:, 0, :, :], o_dir[:, 0, :, :], ALU.mult).then_inc(osq_step, 1)
                dve.wait_ge(osq_step, H * 3 + 2)
                dve.tensor_reduce(orms, o_dir[:, 1, :, :], AX.X, ALU.add).then_inc(osq_step, 1)

            def finish(H):
                dve.wait_ge(orms_done, H + 1)
                dve.reciprocal(orms, orms).then_inc(orms_inv, 1)
                dve.wait_ge(orms_inv, H + 1)
                dve.tensor_tensor(o_dir[:, 0, :, :], o_dir[:, 0, :, :],
                                  orms.unsqueeze(2).broadcast_to([P, NC, P]), ALU.mult).then_inc(oscaled, 1)

            def gate_outputs(H):
                dve.wait_ge(zsilu_done, H + 1)
                for half in range(2):
                    t = slice(HALF * half, HALF * half + HALF)
                    dve.wait_ge(oh_turned, H * 2 + (half + 1))
                    dve.scalar_tensor_tensor(out=oT_h[:, t], in0=psum[2 + half][:, :],
                                             scalar=onorm[:, 0:1], in1=z_silu[:, t], op0=ALU.mult,
                                             op1=ALU.mult).then_inc(gated, 1)

            def layer_b(s):
                W = s * STREAM + B0
                scale(s * 3 + 1, 1, s, True)
                gate_values(s)
                dve.memset(raw[:, :, 0:PAD], 0.0)
                dve.memset(raw[:, :, PAD + S:], 0.0).then_inc(raw_padded, 1)
                wait_alone(dve, passed_dve, gate_act, s * G_ACTS + 9)
                wait_alone(dve, passed_dve, gate_step, s * G_STEPS + G_STEPS)
                take_conv_weights(0, s * DH)
                dve.wait_ge(raw_padded, s + 1)
                for i in range(3):
                    for n in range(2):
                        dve.wait_ge(proj_evicted[n], W + (i + 1 + EV_FREE))
                    convolve(s * DH, i * CONV_K, CONV_K)
                front(0, s * DH, None)
                with dve.Fori(0, DH - 2) as h:
                    head(h, s * DH + h, h * 4 + s * STREAM + (B0 + 4), 2)
                head(DH - 2, s * DH + (DH - 2), s * STREAM + (B0 + B_TILES - 4), 1)
                head(DH - 1, s * DH + (DH - 1), s * STREAM + (B0 + B_TILES), 0)
                for k in range(0, KD, 2):
                    split_even(s * 3 + 2, k)
                add_input(s * 4 + 3, s * 3 + 2, s * STREAM + (B0 + B_TILES))
                scale(s * 3 + 2, 2)

            dve.wait_ge(const_loaded, 16 * N_CONST)
            dve.memset(eps_c[:, 0:1], EPS)
            dve.memset(eps_c[:, 1:2], P * EPS).then_inc(rows_copied, 1)
            for g in range(NG):
                dve.wait_ge(rows_done, g + 1)
                dve.tensor_tensor(rows[:, g, :], psum[g][0:HEADS, 0:REL], outband[:, :],
                                  ALU.add).then_inc(rows_copied, 1)

            with dve.Fori(0, SEQS) as s:
                dve.memset(bias2[0:BAND, :, BAND:P], NEG)
                dve.memset(bias2[BAND:P, :, 0:BAND], NEG).then_inc(q_zeroed, 1)
                dve.memset(q_sb[HD:P, :, 0, :], 0.0)
                dve.memset(q_sb[0:HD, :, 1, :], 0.0).then_inc(q_zeroed, 1)
                for k in range(1, KD):
                    add_square(k, s * 3)
                scale(s * 3, 0, None, True)
                dve.wait_ge(bias_loaded, s * 64 + 64)
                for c in (0, 1):
                    take_out("q", c, SLOTS[0], 0, s * STREAM)
                with dve.Fori(0, PAIRS - 1) as p:
                    pair(s, p, False)
                pair(s, PAIRS - 1, True)
                for k in range(KC_A):
                    dve.wait_ge(o_hi_done, s * 4 + (k + 1))
                    dve.tensor_tensor(h_lo[:, k, :], o_all[:, k, :], h_hi[:, k, :].bitcast(F32),
                                      ALU.subtract).then_inc(o_lo_done, 1)
                add_input(s * 4 + 1, s * 3 + 1, s * STREAM + A_TILES)
                layer_b(s)

        @block.scalar
        def _(act):
            act.sem_inc(w_hi_done, W_FREE)
            act.sem_inc(pt_evicted, PT_FREE)
            act.sem_inc(vt_evicted, V_FREE)

            def square(k, m):
                if k > 2:
                    act.wait_ge(summed, m * (KD - 1) + (k - 2))
                act.activation(sq[:, k % 2, :] if k else sumsq, x_sb[:, k, :],
                               ACT.Square).then_inc(squared, 1)

            def square_sums(m, w0, ahead, n):
                for k in range(O_TILES):
                    if k + ahead < O_TILES:
                        split(w0 + (k + ahead), k % 2, n)
                    for half in range(2):
                        act.wait_ge(proj_evicted[half], w0 + (k + 1 + EV_FREE))
                    square(k, m)

            def rms(m):
                for n in range(2):
                    act.wait_ge(sumsq_done, m * 2 + (n + 1))
                    act.activation(rstd[:, HALF * n:HALF * n + HALF], ps_proj[n][:, :], ACT.Sqrt,
                                   scale=1.0 / D, bias=eps_c[:, 0:1]).then_inc(rms_done, 1)

            def split_h(m):
                for k in range(KD):
                    act.wait_ge(h_scaled, m * KD + (k + 1))
                    act.activation(h_hi[:, k, :], x_sb[:, k, :], ACT.Copy).then_inc(h_hi_done, 1)

            def split(w, b, n=KD * P):
                act.wait_ge(w_loaded[b], w * 8 + (16 - 8 * b))
                act.wait_ge(chain_done, w * 2 + (CH_FREE - 2 * W_BUFS + 2))
                act.activation(w_hi[:, b, 0:n], w_raw[:, b, 0:n], ACT.Copy).then_inc(w_hi_done, 1)

            def take_out(kind, n, g, slot, w):
                act.wait_ge(chain_done, w * 2 + (n + 1 + CH_FREE))
                if kind == "z":
                    act.activation(zs[:, HALF * n:HALF * n + HALF], ps_proj[n][:, :], ACT.Exp,
                                   scale=-1.0).then_inc(z_exp, 1)
                    return
                out, src = in_group_order(k_sb[:, slot, :] if kind == "k" else v_ch, ps_proj[n], g, n)
                act.activation(out, src, ACT.Copy).then_inc(proj_evicted[n], 1)

            def take_values(g, slot, Pn):
                tiles = v_tiles(g)
                act.wait_ge(pv_done, Pn * 24 + (8 * slot + PV_FREE))
                for f in range(0, len(tiles), 4):
                    F = Pn * 8 + (FILL0[slot] + f // 4)
                    bank = ps_v[(FILL0[slot] + f // 4) % 2]
                    act.wait_ge(vt_done, F + 1)
                    part = tiles[f:f + 4]
                    mv = None
                    for a, b in runs([n for _, n in part]):
                        rows_ = part[a][1]
                        mv = act.activation(
                            v_nat[0:rows_, f + a:f + b, :],
                            bank[0:rows_, a * P:b * P].rearrange("p (j c) -> p j c", c=P), ACT.Copy)
                    mv.then_inc(vt_evicted, 1)

            def exponentials(g, slot, t, G):
                _, _, lo, hi = q_tile(g, t)
                act.wait_ge(maxed, G + 1)
                for e in range(2):
                    o = o_sb[:, O_OF[slot], t, :]
                    mv = act.activation(s_sb[:, t % 2, e, lo:hi], s_sb[:, t % 2, e, lo:hi], ACT.Exp,
                                        bias=o[:, P + e:P + e + 1], accum_out=o[:, P + 2 + e:P + 3 + e])
                mv.then_inc(exped, 1)

            def take_probs(g, t, G):
                act.wait_ge(pt_done, G + (1 + S_FREE))
                act.wait_ge(pv_done, G + 1)
                cs = chunks(g, t)
                for a, b in runs([n for _, n, _ in cs]):
                    n = cs[a][1]
                    mv = act.activation(p_t[0:n, t % 2, 2 * a * P:2 * b * P],
                                        ps_pt[0:n, 2 * a * P:2 * b * P], ACT.Copy)
                mv.then_inc(pt_evicted, 1)

            def unit(slot, Pn, w0, par, kinds, gs, slots, per_step, n_split):
                g = SLOTS[slot]
                G0 = Pn * 24 + 8 * slot
                exponentials(g, slot, 0, G0)
                take_values(g, slot, Pn)
                for t in range(QT):
                    take_probs(g, t, G0 + t)
                    if t + 1 < QT:
                        exponentials(g, slot, t + 1, G0 + (t + 1))
                    for c in range(2 * len(kinds)):
                        if evicted_at_step(c, per_step) == t:
                            if kinds[c // 2] in "kvz":
                                take_out(kinds[c // 2], c % 2, gs, slots, w0 + c // 2)
                            if c % 2 and c // 2 < n_split:
                                split(w0 + (c // 2 + 2), (par + c // 2) % 2)

            def pair(s, p, last):
                Pn = s * PAIRS + p
                W = s * STREAM + p * 10
                unit(0, Pn, W + 3, 1, "qkv", SLOTS[1], 1, 18, 3)
                unit(1, Pn, W + 6, 0, "qkv", SLOTS[2], 2, 18, 2 if last else 3)
                if last:
                    unit(2, Pn, W + 9, 1, "z", None, None, 6, 0)
                else:
                    unit(2, Pn, W + 9, 1, "zqk", SLOTS[0], 0, 18, 3)
                act.wait_ge(comb, Pn * 8 + 2)
                act.activation(wgt[:, 1, :, :, :], wgt[:, 1, :, :, :], ACT.Exp).then_inc(comb_exp, 1)
                if not last:
                    for n in range(2):
                        take_out("v", n, SLOTS[0], 0, W + 12)
                    split(W + 14, 0)

            def gate_values(s):
                G = s * G_STEPS
                ab = psum[2][:, 0:NC * 4 * DH].rearrange("p (n c) -> p c n", c=4 * DH)
                act.wait_ge(gate_step, G + 2)
                act.activation(gt[:, 2, :], gt[:, 1, :], ACT.Exp, scale=-1.0).then_inc(gate_act, 1)
                act.activation(gt[:, 3, :].rearrange("p (c n) -> p c n", n=NC), ab[:, DIRS * DH:, :],
                               ACT.Exp, scale=-1.0).then_inc(gate_act, 1)
                act.activation(gt[:, 4, 0:DIRS * DH], a_log[:, :], ACT.Exp).then_inc(gate_act, 1)
                act.wait_ge(gate_step, G + 3)
                act.activation(gt[:, 6, :], gt[:, 5, :], ACT.Ln).then_inc(gate_act, 1)

            def gate_factors(s):
                G = s * G_STEPS
                cum = psum[3][:, 0:P].rearrange("p (d h n) -> p d h n", d=DIRS, h=DH)
                last = psum[3][:, P:2 * P].rearrange("p (d h n) -> p d h n", d=DIRS, h=DH)

                def kind(i):
                    return gates[:, 2 * i:2 * i + 2, :, :]

                act.wait_ge(cum_done, s + 1)
                act.activation(gt[:, 0, :], psum[3][:, 0:P], ACT.Copy).then_inc(gate_act, 1)
                act.activation(kind(EG), cum, ACT.Exp).then_inc(gate_act, 1)
                act.activation(kind(EGL), last, ACT.Exp).then_inc(gate_act, 1)
                act.wait_ge(gate_step, G + 16)
                act.activation(kind(KDX).rearrange("p d h n -> p (d h n)"), gt[:, 1, :],
                               ACT.Exp).then_inc(gate_act, 1)
                act.wait_ge(rows_turned, s + 1)
                act.activation(gt[:, 5, :], psum[4][:, 0:P], ACT.Copy, scale=-1.0).then_inc(gate_act, 1)

            def take_raw(i, n, w):
                act.wait_ge(chain_done, w * 2 + (n + 1 + CH_FREE))
                out = z_raw[:, HALF * n:HALF * (n + 1)] if i == 3 else \
                    raw[:, i, PAD + HALF * n:PAD + HALF * (n + 1)]
                act.activation(out, ps_proj[n][:, :], ACT.Copy).then_inc(proj_evicted[n], 1)

            def silu(H, i):
                act.wait_ge(conv_step, H * (3 * CONV_K) + (i + 1) * CONV_K)
                act.activation(cv[i], cv[i], ACT.Silu).then_inc(silu_done, 1)
                if i < 2:
                    act.wait_ge(silu_done, H * 3 + (i + 1))
                    act.activation(sq_h[:, i, :], cv[i], ACT.Square).then_inc(sq_done, 1)

            def output_rms(H):
                act.wait_ge(osq_step, H * 3 + 3)
                act.activation(orms, orms, ACT.Sqrt, scale=1.0 / P, bias=eps_c[:, 0:1]).then_inc(orms_done, 1)

            def front(H, tail):
                for i in range(2):
                    act.wait_ge(ss_done, H * 2 + (i + 1))
                    act.activation(rnorm[:, i, :], psum[6 + i][:, 0:NC], ACT.Sqrt,
                                   scale=(P, 1.0)[i], bias=eps_c[:, 1 - i:2 - i]).then_inc(rn_sqrt, 1)
                for half in range(2):
                    act.wait_ge(nat_turned, H * 6 + (5 + half))
                    act.activation(vv[:, 1, 4 * half:4 * half + 4, :],
                                   psum[half].rearrange("p (c t) -> p c t", c=4), ACT.Copy).then_inc(vb_out, 1)
                for i in range(2):
                    for half in range(2):
                        act.wait_ge(kq_turned, H * 4 + (2 * i + half + 1))
                        act.activation(kq[:, 4 * half:4 * half + 4, 1 - i, :],
                                       psum[2 + 2 * i + half].rearrange("p (c t) -> p c t", c=4),
                                       ACT.Copy).then_inc(kq_out, 1)
                act.wait_ge(d_added, H * 2 + 2)
                for c in range(NC):
                    for d in range(DIRS):
                        mv = act.activation(decay[:, 2 * c + d, :], decay[:, 2 * c + d, :], ACT.Exp,
                                            bias=gate_h[:, GSGN, d, c:c + 1])
                    if c % 2:
                        mv.then_inc(d_exped, 1)
                if tail is not None:
                    output_rms(tail)
                for half in range(2):
                    act.wait_ge(qkt_turned, H * 2 + (half + 1))
                    act.activation(qkt[:, 8 * half:8 * half + 8, :].rearrange("p (c d) t -> p c d t", d=2)[:, :, 0, :],
                                   psum[4 + half].rearrange("p (c t) -> p c t", c=4),
                                   ACT.Copy).then_inc(qkt_out, 1)

            def fill_front(Wn):
                for i in range(3):
                    for n in range(2):
                        take_raw(i, n, Wn + i)
                    if i < 2:
                        split(Wn + (i + 2), i)

            def head(H, Wn, more):
                act.wait_ge(gated, H * 2 + HEAD_FREE)
                for n in range(2):
                    act.wait_ge(proj_evicted[n], Wn + EV_FREE)
                act.activation(z_silu, z_raw, ACT.Silu).then_inc(zsilu_done, 1)

                def take_group(g, made, base, dst, out):
                    act.wait_ge(made, H * 4 + (g + 1))
                    act.activation(dst[:, 4 * g:4 * g + 4, :],
                                   psum[base + g % 2].rearrange("p (j t) -> p j t", j=4),
                                   ACT.Copy).then_inc(out, 1)

                for g in range(4):
                    take_group(g, inv_turned, 6, inv_t, inv_t_out)
                act.wait_ge(heads_stored, H * 16 + HEAD_FREE)
                for g in range(4):
                    take_group(g, x1_made, 2, xm, x1_out)
                for g in range(4):
                    take_group(g, x2_made, 2, xm, x2_out)
                if more:
                    silu(H + 1, 0)
                    silu(H + 1, 1)
                    split(Wn + 4, 0)
                for i in range(NC):
                    if i:
                        for d in range(DIRS):
                            c = (i, NC - 1 - i)[d]
                            act.wait_ge(qs_made[d], H * (NC - 1) + i)
                            act.activation(o_dir[:, d, c, :], psum[4 + d][:, 0:P], ACT.Copy,
                                           scale=gate_h[:, EG, d, c:c + 1]).then_inc(qs_out[d], 1)
                    for d in range(DIRS):
                        c = (i, NC - 1 - i)[d]
                        act.wait_ge(vn_made[d], H * NC + (i + 1))
                        if d:
                            act.activation(v_new[:, 1, :], psum[5][:, 0:P], ACT.Copy,
                                           scale=gate_h[:, BETA, 1, c:c + 1]).then_inc(vn_out[1], 1)
                        else:
                            act.activation(v_new[:, 0, :], psum[4][:, 0:P],
                                           ACT.Copy).then_inc(vn_out[0], 1)
                    if more and i % 4 == 3:
                        take_raw(3, i // 4, Wn + 3)
                    if more and i == 6:
                        silu(H + 1, 2)
                if more:
                    split(Wn + 5, 1)
                    front(H + 1, H)
                else:
                    output_rms(H)
                if more > 1:
                    fill_front(Wn + 4)

            def layer_b(s):
                W = s * STREAM + B0
                split(W, 0)
                split(W + 1, 1)
                rms(s * 3 + 1)
                split_h(s * 3 + 1)
                gate_values(s)
                for i in range(4):
                    for n in range(2):
                        take_raw(i, n, W + i)
                    split(W + (i + 2), i % 2)
                    if i == 0:
                        gate_factors(s)
                for i in range(3):
                    silu(s * DH, i)
                front(s * DH, None)
                fill_front(W + 4)
                with act.Fori(0, DH - 2) as h:
                    head(s * DH + h, h * 4 + s * STREAM + (B0 + 4), 2)
                head(s * DH + (DH - 2), s * STREAM + (B0 + B_TILES - 4), 1)
                head(s * DH + (DH - 1), s * STREAM + (B0 + B_TILES), 0)
                for k in range(KD):
                    act.wait_ge(x_loaded[k], s * 64 + 48)
                    act.activation(h_hi[:, k, :], x_sb[:, k, :], ACT.Copy).then_inc(h_hi_done, 1)
                square_sums(s * 3 + 2, s * STREAM + (B0 + B_TILES), 2, KD * P)
                rms(s * 3 + 2)

            with act.Fori(0, SEQS) as s:
                act.wait_ge(rows_copied, 1)
                for k in range(KD):
                    act.wait_ge(x_loaded[k], s * 64 + 16)
                    square(k, s * 3)
                W = s * STREAM
                split(W, 0)
                split(W + 1, 1)
                rms(s * 3)
                split_h(s * 3)
                for tau in range(3):
                    for n in range(2):
                        if tau:
                            take_out("-kv"[tau], n, SLOTS[0], 0, W + tau)
                    split(W + (tau + 2), tau % 2)
                with act.Fori(0, PAIRS - 1) as p:
                    pair(s, p, False)
                pair(s, PAIRS - 1, True)
                for k in range(KC_A):
                    act.wait_ge(ot_evicted, s * (2 * PAIRS) + (2 * PAIRS + OT_FREE))
                    act.activation(h_hi[:, k, :], o_all[:, k, :], ACT.Copy).then_inc(o_hi_done, 1)
                for j in range(2):
                    split(s * STREAM + (A_TILES + j), j, KC_A * P)
                square_sums(s * 3 + 1, s * STREAM + A_TILES, 2, KC_A * P)
                layer_b(s)

        @block.gpsimd
        def _(pool):
            pool.sem_inc(w_lo_done, W_FREE)

            def split(w, b, n=KD * P):
                pool.wait_ge(w_hi_done, w + (1 + W_FREE))
                pool.tensor_tensor(w_lo[:, b, 0:n], w_raw[:, b, 0:n], w_hi[:, b, 0:n].bitcast(F32),
                                   ALU.subtract).then_inc(w_lo_done, 1)

            def split_odd(m):
                for k in range(1, KD, 2):
                    pool.wait_ge(h_hi_done, m * KD + (k + 1))
                    pool.tensor_tensor(h_lo[:, k, :], x_sb[:, k, :], h_hi[:, k, :].bitcast(F32),
                                       ALU.subtract).then_inc(h_lo_pool, 1)

            def add_masks(H):
                pool.wait_ge(gates_loaded, H * 32 + 32)
                for d in range(DIRS):
                    view = decay.rearrange("p (c d) t -> p c d t", d=DIRS)[:, :, d, :]
                    pool.tensor_tensor(view, view, masks[:, 0:1, :].broadcast_to([P, NC, P]),
                                       ALU.add).then_inc(d_added, 1)

            def front(H, Wn, tail, fill):
                pool.wait_ge(head_set, H + 1)
                pool.wait_ge(nat_out, H * 4 + 4)
                for d in range(DIRS):
                    pool.tensor_tensor(kdec[:, d, :, :], nat[:, 1, :, :],
                                       gate_h[:, KDX, d, :].unsqueeze(2).broadcast_to([P, NC, P]),
                                       ALU.mult).then_inc(kdec_done, 1)
                pool.wait_ge(low_done, H * 4 + 4)
                if tail:
                    pool.wait_ge(oh_turned, H * 2)
                pool.tensor_tensor(low1, low, masks[:, 1:2, :].broadcast_to([P, NU, P]),
                                   ALU.mult).then_inc(low1_done, 1)
                if fill:
                    split(Wn + 2, 0)
                pool.wait_ge(low1_done, H + 1)
                pool.wait_ge(blocks_stored, H * 64 + 64)
                pool.tensor_tensor(low, low, masks[:, 2:3, :].broadcast_to([P, NU, P]),
                                   ALU.mult).then_inc(low2_done, 1)
                if fill:
                    split(Wn + 3, 1)

            def head(H, Wn, more):
                if more:
                    split(Wn + 4, 0)
                    add_masks(H + 1)
                    split(Wn + 5, 1)
                    front(H + 1, Wn + 4, True, more > 1)

            def layer_b(s):
                W = s * STREAM + B0
                for i in range(2):
                    split(W + i, i % 2)
                split_odd(s * 3 + 1)
                for i in range(2, 6):
                    split(W + i, i % 2)
                add_masks(s * DH)
                front(s * DH, W + 4, False, True)
                with pool.Fori(0, DH - 2) as h:
                    head(s * DH + h, h * 4 + s * STREAM + (B0 + 4), 2)
                head(s * DH + (DH - 2), s * STREAM + (B0 + B_TILES - 4), 1)
                split_odd(s * 3 + 2)
                for i in range(2, O_TILES):
                    split(s * STREAM + (B0 + B_TILES + i), i % 2)

            with pool.Fori(0, SEQS) as s:
                W = s * STREAM
                for tau in range(2):
                    split(W + tau, tau % 2)
                split_odd(s * 3)
                for tau in range(2, 5):
                    split(W + tau, tau % 2)
                with pool.Fori(0, PAIRS - 1) as p:
                    W = s * STREAM + p * 10
                    for i in range(9):
                        split(W + (5 + i), (1 + i) % 2)
                    combine_pool(pool, s * PAIRS + p)
                    split(W + 14, 0)
                W = s * STREAM + 30
                for i in range(5):
                    split(W + (5 + i), (1 + i) % 2)
                combine_pool(pool, s * PAIRS + 3)
                with pool.Fori(0, O_TILES // 2) as i:
                    for j in range(2):
                        split(s * STREAM + i * 2 + (A_TILES + j), j, KC_A * P)
                layer_b(s)

        @block.sync
        def _(sp):
            sp.sem_inc(xch_written, XW_FREE)
            sp.sem_inc(heads_stored, HEAD_FREE)
            for dst, src in consts:
                sp.dma_start(dst, src).then_inc(const_loaded, 16)

            def load_w(w, tau, b, src=wA):
                wait_alone(sp, passed_sp, w_hi_done, w + (1 + W_FREE - W_BUFS))
                wait_alone(sp, passed_sp, w_lo_done, w + (1 + W_FREE - W_BUFS))
                sp.dma_start(w_raw[:, b, :], src[tau]).then_inc(w_loaded[b], 16)

            def load_x(src):
                for k in range(KD):
                    sp.dma_start(x_sb[:, k, :], src[:, k, :]).then_inc(x_loaded[k], 16)

            for j in range(2):
                load_w(j, j, j)
            load_x(xT[0])
            sp.wait_ge(rows_copied, NG + 1)
            sp.dma_start(bias_rows.ap().rearrange("(g h) r -> h g r", g=NG), rows[:, :, :]).then_inc(rows_stored, 16)
            sp.wait_ge(rows_stored, 16)
            sp.dma_start(bias_copies.ap(), bass.AP(bias_rows, 0, [[REL, NG * HEADS], [0, P], [1, REL]])).then_inc(rows_copied_out, 16)
            sp.wait_ge(rows_copied_out, 16)

            def load_bias(s):
                wait_alone(sp, passed_sp, q_zeroed, s * 2 + 1)
                for g in range(2):
                    sp.dma_start(bias01[g], bass.AP(bias_copies, g * HEADS * P * REL + REL0 - BAND,
                                                    [[REL - 1, P], [P * REL, HEADS], [1, 4 * BAND]])).then_inc(bias_loaded, 16)
                for half in range(2):
                    r = slice(BAND * half, BAND * half + BAND)
                    sp.dma_start(bias2[r, :, r], bass.AP(bias_copies, 2 * HEADS * P * REL + REL0,
                                                         [[REL - 1, BAND], [P * REL, HEADS], [1, BAND]])).then_inc(bias_loaded, 16)

            def exchange(Pn, slot):
                if slot == 0:
                    wait_alone(sp, passed_sp, o_evicted, Pn * 24 + (8 + O_FREE))
                    sp.dma_start(xch[0].rearrange("(b p r) c -> p r b c", b=2, p=P),
                                 o_sb[:, 3, :, :].rearrange("p (r b) c -> p r b c", b=2)).then_inc(xch_written, 16)
                    wait_alone(sp, passed_sp, xch_written, Pn * 48 + (16 + XW_FREE))
                    sp.dma_start(o_sb[:, 1, :, :], xch[0].rearrange("(t p) c -> p t c", p=P)).then_inc(xch_read, 16)
                    wait_alone(sp, passed_sp, xch_read, Pn * 32 + 16)
                else:
                    wait_alone(sp, passed_sp, o_evicted, Pn * 24 + (16 + O_FREE))
                    for h in range(2):
                        sp.dma_start(xch[1].rearrange("(l t h) c -> h l t c", t=QT, h=2)[h],
                                     o_sb[HD * h:HD * h + HD, 2, :, :]).then_inc(xch_written, 16)
                    wait_alone(sp, passed_sp, xch_written, Pn * 48 + (48 + XW_FREE))
                    sp.dma_start(o_sb[:, 2, :, :], xch[1].rearrange("(t p) c -> p t c", p=P)).then_inc(xch_read, 16)
                    wait_alone(sp, passed_sp, xch_read, Pn * 32 + 32)

            def load_out_a(w, tau):
                b = tau % 2
                wait_alone(sp, passed_sp, w_hi_done, w + (1 + W_FREE - W_BUFS))
                wait_alone(sp, passed_sp, w_lo_done, w + (1 + W_FREE - W_BUFS))
                sp.dma_start(w_raw[:, b, 0:KC_A * P], woA[tau]).then_inc(w_loaded[b], 16)

            def load_rows(h):
                for d in range(DIRS):
                    row = gate_rows[bass.ds(h + d * DH, 1), :, :]
                    sp.dma_start(decay.rearrange("p (c d) t -> p c d t", d=DIRS)[:, :, d, :],
                                 row.broadcast_to([P, NC, P])).then_inc(gates_loaded, 16)

            def load_pair(Wn, tau):
                for j in range(2):
                    load_w(Wn + j, tau + j, j, wB)

            def front(H, tail=None):
                wait_alone(sp, passed_sp, low_done, H * 4 + 4)
                for b in range(NB):
                    r = slice(BLK * b, BLK * b + BLK)
                    sp.dma_start(blocks[b].rearrange("u i j -> i u j"), low[r, :, r]).then_inc(blocks_stored, 16)
                wait_alone(sp, passed_sp, blocks_stored, H * 64 + 64)
                sp.dma_start(lanes[0:LANES, :, :], blocks.rearrange("b u i j -> (b u) i j")).then_inc(lanes_loaded, 16)
                wait_alone(sp, passed_sp, sub_done, H + 1)
                sp.dma_start(inverses.rearrange("b u i j -> (b u) i j"), lanes[0:LANES, :, :]).then_inc(inverses_stored, 16)
                if tail is not None:
                    store_head(*tail)
                wait_alone(sp, passed_sp, inverses_stored, H * 16 + 16)
                wait_alone(sp, passed_sp, inv_zeroed, H + 1)
                for b in range(NB):
                    r = slice(BLK * b, BLK * b + BLK)
                    sp.dma_start(inv[r, :, r], inverses[b].rearrange("u i j -> i u j")).then_inc(inv_loaded, 16)

            def store_head(h, H):
                wait_alone(sp, passed_sp, gated, H * 2 + (2 + HEAD_FREE))
                sp.dma_start(headsT[bass.ds(h, 1), :, :].rearrange("a p t -> p (a t)"), oT_h).then_inc(heads_stored, 16)

            def head(h, H, Wn, tau, more):
                if more:
                    wait_alone(sp, passed_sp, fin_out, H * 4 + 4)
                    load_rows(h + 1)
                    load_pair(Wn + 6, tau + 6)
                    front(H + 1, (h, H))
                    if more > 1:
                        load_pair(Wn + 8, tau + 8)
                else:
                    store_head(h, H)

            def layer_b(s):
                W = s * STREAM + B0
                for k in range(KD):
                    wait_alone(sp, passed_sp, proj_evicted[0], s * STREAM + (A_TILES + k + 1 + EV_FREE))
                    wait_alone(sp, passed_sp, proj_evicted[1], s * STREAM + (A_TILES + k + 1 + EV_FREE))
                    sp.dma_start(x1T[s][:, k, :], x_sb[:, k, :]).then_inc(x_stored[k], 16)
                    if k == KD - 3:
                        for j in range(2):
                            load_w(W + j, j, j, wB)
                for j in range(2, 4):
                    load_w(W + j, j, j % 2, wB)
                wait_alone(sp, passed_sp, gate_act, s * G_ACTS + 9)
                sp.dma_start(gate_rows.rearrange("g n t -> (g n) t"), gt[:, 5, :]).then_inc(rows_out, 16)
                wait_alone(sp, passed_sp, rows_out, s * 16 + 16)
                wait_alone(sp, passed_sp, h_lo_dve, s * 12 + 8)
                wait_alone(sp, passed_sp, h_lo_pool, s * 12 + 8)
                load_rows(0)
                load_pair(W + 4, 4)
                load_pair(W + 6, 6)
                front(s * DH)
                load_pair(W + 8, 8)
                with sp.Fori(0, DH - 2) as h:
                    head(h, s * DH + h, h * 4 + s * STREAM + (B0 + 4), h * 4 + 4, 2)
                head(DH - 2, s * DH + (DH - 2), s * STREAM + (B0 + B_TILES - 4), B_TILES - 4, 1)
                head(DH - 1, s * DH + (DH - 1), s * STREAM + (B0 + B_TILES), B_TILES, 0)
                wait_alone(sp, passed_sp, heads_stored, s * (16 * DH) + (16 * DH + HEAD_FREE))
                load_x(headsT.rearrange("h p t -> p h t"))

                for k in range(KD):
                    wait_alone(sp, passed_sp, h_lo_pool if k % 2 else h_lo_dve, s * 12 + (8 + k // 2 + 1))
                    sp.dma_start(x_sb[:, k, :], x1T[s][:, k, :]).then_inc(x_loaded[k], 16)
                for j in range(4, O_TILES):
                    load_w(W + (B_TILES + j), B_TILES + j, j % 2, wB)
                for k in range(KD):
                    wait_alone(sp, passed_sp, h_scaled, s * (3 * KD) + (2 * KD + k + 1))
                    sp.dma_start(yT[s][:, k, :], x_sb[:, k, :]).then_inc(x_stored[k], 16)

            def sequence(s):
                load_bias(s)
                W = s * STREAM
                for tau in range(2, 6):
                    load_w(W + tau, tau, tau % 2)
                with sp.Fori(0, PAIRS - 1) as p:
                    W = s * STREAM + p * 10
                    for i in range(3):
                        load_w(W + (6 + i), p * 10 + (6 + i), i % 2)
                    exchange(s * PAIRS + p, 0)
                    for i in range(3):
                        load_w(W + (9 + i), p * 10 + (9 + i), (1 + i) % 2)
                    exchange(s * PAIRS + p, 1)
                    for i in range(4):
                        load_w(W + (12 + i), p * 10 + (12 + i), i % 2)
                W = s * STREAM + 30
                for i in range(3):
                    load_w(W + (6 + i), 36 + i, i % 2)
                exchange(s * PAIRS + 3, 0)
                load_w(W + 9, 39, 1)
                exchange(s * PAIRS + 3, 1)
                for j in range(2):
                    load_out_a(s * STREAM + (A_TILES + j), j)
                wait_alone(sp, passed_sp, ot_done, s * (2 * PAIRS) + 2 * PAIRS)
                load_x(xT[s])
                for j in range(2, O_TILES):
                    load_out_a(s * STREAM + (A_TILES + j), j)
                layer_b(s)

            with sp.Fori(0, SEQS - 1) as s:
                sequence(s)
                for j in range(2):
                    load_w(s * STREAM + (STREAM + j), j, j)
                for k in range(KD):
                    wait_alone(sp, passed_sp, x_stored[k], s * 32 + 32)
                    sp.dma_start(x_sb[:, k, :], xT[s + 1][:, k, :]).then_inc(x_loaded[k], 16)
            sequence(SEQS - 1)
            for k in range(KD):
                sp.wait_ge(x_stored[k], 32 * SEQS)


def t5_bucket(rel):
    nb = NUM_BUCKETS // 2
    exact = nb // 2
    n = np.abs(rel)
    large = exact + (np.log(np.maximum(n, 1) / exact) / np.log(1024 / exact)
                     * (nb - exact)).astype(np.int32)
    large = np.minimum(large, nb - 1)
    return (rel > 0).astype(np.int32) * nb + np.where(n < exact, n, large).astype(np.int32)


def kernel(x_prompt, x_sample, norm_w, final_norm_w, rel_bias, a_w_in, a_w_out, b_w_in,
           b_conv_w, b_A_log, b_dt_bias, b_out_norm_w, b_w_out):
    import concourse.bacc as bacc
    from concourse.bass_utils import run_bass_kernel_spmd

    def channel_tiles(w):
        r, c = w.shape
        return np.ascontiguousarray(w.reshape(r // P, P, c // P, P).transpose(2, 1, 0, 3))

    x = np.stack([np.asarray(x_prompt)[0], np.asarray(x_sample)[0]])
    xT = np.ascontiguousarray(x.reshape(SEQS, S, KD, P).transpose(0, 3, 2, 1))
    base = channel_tiles(np.asarray(a_w_in)[0])

    def tile(g, which, p):
        return 4 * (3 * g + which) + p

    order = [tile(SLOTS[0], j, 0) for j in range(3)]
    for p in range(PAIRS):
        for slot in (1, 2):
            order += [tile(SLOTS[slot], j, p) for j in range(3)]
        order.append(36 + p)
        if p + 1 < PAIRS:
            order += [tile(SLOTS[0], j, p + 1) for j in range(3)]
    wA = np.ascontiguousarray(base[order]).reshape(A_TILES, P, KD * P)
    woA = channel_tiles(np.asarray(a_w_out)[0]).reshape(O_TILES, P, KC_A * P)
    w_in = np.asarray(b_w_in)[0]
    base = channel_tiles(w_in[:, :4 * D])
    order = [i * DH + h for h in range(DH) for i in range(4)]
    wB = np.concatenate([base[order], channel_tiles(np.asarray(b_w_out)[0])]).reshape(-1, P, KD * P)
    wab = np.ascontiguousarray(w_in[:, 4 * D:].reshape(KD, P, 4 * DH).transpose(1, 0, 2))
    conv_w = np.ascontiguousarray(np.asarray(b_conv_w)[0].reshape(CONV_K, 3, DH, P).transpose(3, 1, 2, 0))

    def on_all(v):
        return np.ascontiguousarray(np.broadcast_to(np.asarray(v).reshape(1, -1), (P, v.size)))

    i, j = np.arange(P)[:, None], np.arange(P)[None, :]
    tri = np.stack([i <= j, i >= j], 1).astype(np.float32)
    merge = [(i // m == j // m + 1) & (i // m % 2 == 1) for m in (BLK, 2 * BLK)]
    masks = np.stack([np.where(i >= j, 0.0, NEG), *merge], 1).astype(np.float32)
    nw = np.concatenate([np.asarray(norm_w), np.asarray(final_norm_w)[None]])
    nw = np.ascontiguousarray(nw.reshape(3, KD, P).transpose(2, 0, 1))
    rel = np.arange(REL) - REL0
    onehot = np.zeros((NUM_BUCKETS, NG, REL), np.float32)
    for g, (_, dil) in enumerate(GROUPS):
        inside = np.abs(rel) <= BAND
        onehot[t5_bucket(rel * dil)[inside], g, np.nonzero(inside)[0]] = 1.0
    outband = np.broadcast_to(np.where(np.abs(rel) <= BAND, 0.0, NEG), (HEADS, REL)).astype(np.float32)
    arrays = {"xT": xT, "wA": wA, "woA": woA, "wB": wB, "norm_w": nw, "rel_bias": np.asarray(rel_bias),
              "onehot": onehot, "outband": np.ascontiguousarray(outband),
              "ident": np.eye(P, dtype=np.float32), "ones": np.ones((P, P), np.float32),
              "conv_w": conv_w, "wab": wab, "a_log": on_all(np.asarray(b_A_log)[0]),
              "dt": on_all(np.asarray(b_dt_bias)[0]),
              "onorm": np.ascontiguousarray(np.asarray(b_out_norm_w)[0][:, None]),
              "tri": tri, "masks": masks}
    nc = bacc.Bacc("TRN2", target_bir_lowering=False, num_devices=1)
    args = [nc.dram_tensor("d_" + n, a.shape, F32, kind="ExternalInput").ap() for n, a in arrays.items()]
    out = nc.dram_tensor("y_out", xT.shape, F32, kind="ExternalOutput").ap()
    program(nc, *args, out)
    r = run_bass_kernel_spmd(nc, [{"d_" + n: a for n, a in arrays.items()}], core_ids=[0])
    y = np.asarray(r.results[0]["y_out"]).transpose(0, 3, 2, 1).reshape(SEQS, S, D)
    return y[0:1], y[1:2]
```
